# Optimizing a Trainium2 kernel written in Bass

```python
import jax, jax.numpy as jnp
from jax import lax
import numpy as np
import jax
import jax.numpy as jnp

D_MODEL = 2048
BATCH = 1
SEQ = 256
DEPTH = 1

MIX_WIDTH = D_MODEL
HEAD_DIM = 128
DELTA_WIDTH = MIX_WIDTH // 2
N_DELTA_HEADS = DELTA_WIDTH // HEAD_DIM
DILATED_WIDTH = MIX_WIDTH - DELTA_WIDTH
N_DILATED_HEADS = DILATED_WIDTH // HEAD_DIM
DILATION_PAIRS = ((128, 1), (512, 4), (2048, 16))
N_BRANCH = 3
ATTN_BLOCK = 128
DELTA_CHUNK = 64
SHORT_CONV_WIDTH = 5
FFN_CONV_WIDTH = 3
D_FF = 5632
ROPE_THETA = 500000.0
ROT_DIM = HEAD_DIM // 4
NORM_EPS = 1e-6
NEG_INF = -1e30
PROJ_WIDTH = 4 * DELTA_WIDTH + 4 * N_DELTA_HEADS + 3 * N_BRANCH * DILATED_WIDTH


def rms_norm(x, w):
    xf = x.astype(jnp.float32)
    y = xf * lax.rsqrt(jnp.mean(xf * xf, axis=-1, keepdims=True) + NORM_EPS)
    return (y * w.astype(jnp.float32)).astype(x.dtype)

def l2_normalize(x):
    return x * lax.rsqrt(jnp.sum(x * x, axis=-1, keepdims=True) + NORM_EPS)

def depthwise_conv_centered(x, w):
    width, ch = w.shape
    return lax.conv_general_dilated(
        x, w[:, None, :].astype(x.dtype), window_strides=(1,),
        padding=[(width // 2, width // 2)],
        dimension_numbers=("NWC", "WIO", "NWC"), feature_group_count=ch)

def partial_rope(x, positions):
    inv_freq = ROPE_THETA ** (-jnp.arange(0, ROT_DIM, 2, dtype=jnp.float32) / ROT_DIM)
    ang = positions.astype(jnp.float32)[..., None] * inv_freq
    cos = jnp.cos(ang)[:, :, None, :]
    sin = jnp.sin(ang)[:, :, None, :]
    xr = x[..., :ROT_DIM].astype(jnp.float32)
    x1, x2 = xr[..., :ROT_DIM // 2], xr[..., ROT_DIM // 2:]
    rot = jnp.concatenate([x1 * cos - x2 * sin, x2 * cos + x1 * sin], axis=-1)
    return jnp.concatenate([rot.astype(x.dtype), x[..., ROT_DIM:]], axis=-1)

def gated_delta_chunked(q, k, v, g, beta):
    bsz, nh, s, dk = q.shape
    dv = v.shape[-1]
    c = DELTA_CHUNK
    n = s // c
    q = q.reshape(bsz, nh, n, c, dk)
    k = k.reshape(bsz, nh, n, c, dk)
    v = v.reshape(bsz, nh, n, c, dv)
    g = g.reshape(bsz, nh, n, c)
    beta = beta.reshape(bsz, nh, n, c)
    cum_g = jnp.cumsum(g, axis=-1)
    lower = np.tril(np.ones((c, c), dtype=bool))
    strict = np.tril(np.ones((c, c), dtype=bool), -1)
    gamma = jnp.exp(jnp.where(lower, cum_g[..., :, None] - cum_g[..., None, :], NEG_INF))
    k_beta = k * beta[..., None]
    a_mat = jnp.where(strict, jnp.einsum("bhnik,bhnjk->bhnij", k_beta, k) * gamma, 0.0)
    t_mat = a_mat + jnp.eye(c, dtype=jnp.float32)
    u = lax.linalg.triangular_solve(t_mat, v * beta[..., None], left_side=True,
                                    lower=True, unit_diagonal=True)
    w = lax.linalg.triangular_solve(t_mat, k_beta * jnp.exp(cum_g)[..., None], left_side=True,
                                    lower=True, unit_diagonal=True)
    qk = jnp.einsum("bhnik,bhnjk->bhnij", q, k) * gamma
    q_dec = q * jnp.exp(cum_g)[..., None]
    k_tail = k * jnp.exp(cum_g[..., -1:] - cum_g)[..., None]
    chunk_decay = jnp.exp(cum_g[..., -1])

    def step(state, xs):
        u_n, w_n, qd_n, qk_n, kt_n, dec_n = xs
        v_new = u_n - jnp.einsum("bhck,bhkv->bhcv", w_n, state)
        o_n = (jnp.einsum("bhck,bhkv->bhcv", qd_n, state)
               + jnp.einsum("bhcj,bhjv->bhcv", qk_n, v_new))
        state = state * dec_n[..., None, None] + jnp.einsum("bhck,bhcv->bhkv", kt_n, v_new)
        return state, o_n

    xs = tuple(jnp.moveaxis(t, 2, 0) for t in (u, w, q_dec, qk, k_tail, chunk_decay))
    state0 = jnp.zeros((bsz, nh, dk, dv), jnp.float32)
    _, o = lax.scan(step, state0, xs)
    return jnp.moveaxis(o, 0, 2).reshape(bsz, nh, s, dv)

def delta_mixer(qkv_raw, z, a_f, a_b, b_f, b_b, conv_w, a_log_f, a_log_b, dt_b_f, dt_b_b, norm_w):
    bsz, s, _ = qkv_raw.shape
    qkv = jax.nn.silu(depthwise_conv_centered(qkv_raw, conv_w))
    q, k, v = jnp.split(qkv.astype(jnp.float32), 3, axis=-1)
    to_heads = lambda t: t.reshape(bsz, s, N_DELTA_HEADS, HEAD_DIM).transpose(0, 2, 1, 3)
    q = l2_normalize(to_heads(q)) * (HEAD_DIM ** -0.5)
    k = l2_normalize(to_heads(k))
    v = to_heads(v)

    def gates(a, b, a_log, dt_bias):
        a = a.astype(jnp.float32).transpose(0, 2, 1)
        b = b.astype(jnp.float32).transpose(0, 2, 1)
        g = -jnp.exp(a_log.astype(jnp.float32))[:, None] * jax.nn.softplus(
            a + dt_bias.astype(jnp.float32)[:, None])
        return g, jax.nn.sigmoid(b)

    g_f, beta_f = gates(a_f, b_f, a_log_f, dt_b_f)
    g_b, beta_b = gates(a_b, b_b, a_log_b, dt_b_b)
    flip = lambda t: jnp.flip(t, axis=2)
    o = (gated_delta_chunked(q, k, v, g_f, beta_f)
         + flip(gated_delta_chunked(flip(q), flip(k), flip(v), flip(g_b), flip(beta_b))))
    o = o.transpose(0, 2, 1, 3)
    o = o * lax.rsqrt(jnp.mean(o * o, axis=-1, keepdims=True) + NORM_EPS) * norm_w.astype(jnp.float32)
    o = o * jax.nn.silu(z.astype(jnp.float32).reshape(bsz, s, N_DELTA_HEADS, HEAD_DIM))
    return o.reshape(bsz, s, DELTA_WIDTH)

def dilated_window_attention(q, k, v, dilation, half_span):
    bsz, nh, s, dh = q.shape
    length = s // dilation
    nb = -(-length // ATTN_BLOCK)
    lp = nb * ATTN_BLOCK
    span = ATTN_BLOCK + 2 * half_span
    by_residue = lambda t: t.reshape(bsz, nh, length, dilation, dh).transpose(0, 1, 3, 2, 4)
    pad_q = ((0, 0), (0, 0), (0, 0), (0, lp - length), (0, 0))
    pad_kv = ((0, 0), (0, 0), (0, 0), (half_span, lp - length + half_span), (0, 0))
    qb = jnp.pad(by_residue(q), pad_q).reshape(bsz, nh, dilation, nb, ATTN_BLOCK, dh)
    idx = (np.arange(nb) * ATTN_BLOCK)[:, None] + np.arange(span)[None, :]
    kb = jnp.take(jnp.pad(by_residue(k), pad_kv), idx, axis=3)
    vb = jnp.take(jnp.pad(by_residue(v), pad_kv), idx, axis=3)
    scores = jnp.einsum("bhrnqe,bhrnke->bhrnqk", qb, kb,
                        preferred_element_type=jnp.float32) * (dh ** -0.5)
    qpos = (np.arange(nb) * ATTN_BLOCK)[:, None] + np.arange(ATTN_BLOCK)[None, :]
    kpos = (np.arange(nb) * ATTN_BLOCK - half_span)[:, None] + np.arange(span)[None, :]
    rel = kpos[:, None, :] - qpos[:, :, None]
    mask = (np.abs(rel) <= half_span) & (kpos[:, None, :] >= 0) & (kpos[:, None, :] < length)
    scores = jnp.where(mask, scores, NEG_INF)
    m = jnp.max(scores, axis=-1, keepdims=True)
    p = jnp.exp(scores - m)
    denom = jnp.sum(p, axis=-1, keepdims=True)
    o = jnp.einsum("bhrnqk,bhrnke->bhrnqe", p, vb.astype(jnp.float32)) / denom
    lse = (m + jnp.log(denom))[..., 0]
    o = o.reshape(bsz, nh, dilation, lp, dh)[:, :, :, :length]
    o = o.transpose(0, 1, 3, 2, 4).reshape(bsz, nh, s, dh)
    lse = lse.reshape(bsz, nh, dilation, lp)[:, :, :, :length].transpose(0, 1, 3, 2).reshape(bsz, nh, s)
    return o, lse

def dilated_mixer(bq, bk, bv, positions):
    bsz, s, _ = bq.shape
    outs, lses = [], []
    for gi, (window, dilation) in enumerate(DILATION_PAIRS):
        sl = slice(gi * DILATED_WIDTH, (gi + 1) * DILATED_WIDTH)
        heads = lambda t: t[..., sl].reshape(bsz, s, N_DILATED_HEADS, HEAD_DIM)
        q = partial_rope(heads(bq), positions).transpose(0, 2, 1, 3)
        k = partial_rope(heads(bk), positions).transpose(0, 2, 1, 3)
        v = heads(bv).transpose(0, 2, 1, 3)
        o, lse = dilated_window_attention(q, k, v, dilation, window // (2 * dilation))
        outs.append(o)
        lses.append(lse)
    weights = jax.nn.softmax(jnp.stack(lses, axis=0), axis=0)
    o = jnp.sum(weights[..., None] * jnp.stack(outs, axis=0), axis=0)
    return o.transpose(0, 2, 1, 3).reshape(bsz, s, DILATED_WIDTH)

def token_mixer(n, positions, w_in, conv_qkv_w, a_log_f, a_log_b, dt_b_f, dt_b_b, delta_norm_w, w_out):
    proj = jnp.einsum("bsd,dp->bsp", n, w_in)
    sizes = [3 * DELTA_WIDTH, DELTA_WIDTH] + [N_DELTA_HEADS] * 4 + [N_BRANCH * DILATED_WIDTH] * 3
    splits = [int(i) for i in np.cumsum(sizes)[:-1]]
    qkv_a, z, a_f, a_b, b_f, b_b, bq, bk, bv = jnp.split(proj, splits, axis=-1)
    out_a = delta_mixer(qkv_a, z, a_f, a_b, b_f, b_b, conv_qkv_w,
                        a_log_f, a_log_b, dt_b_f, dt_b_b, delta_norm_w)
    out_b = dilated_mixer(bq, bk, bv, positions)
    mixed = jnp.concatenate([out_a, out_b], axis=-1).astype(n.dtype)
    return jnp.einsum("bsm,md->bsd", mixed, w_out)

def conv_gated_mlp(n, w_ffn_in, conv_ffn_w, w_ffn_out):
    up = depthwise_conv_centered(jnp.einsum("bsd,df->bsf", n, w_ffn_in), conv_ffn_w)
    gate, val = jnp.split(up, 2, axis=-1)
    return jnp.einsum("bsf,fd->bsd", jax.nn.silu(gate) * val, w_ffn_out)

def first_inputs(seed: int = 0) -> dict:
    key = jax.random.key(seed)
    ks = jax.random.split(key, 16)
    f32 = jnp.float32
    nrm = lambda k, shape, scale: jax.random.normal(k, shape, f32) * scale
    gain = lambda k, shape: 1.0 + 0.02 * jax.random.normal(k, shape, f32)

    def dt_bias(k):
        dt = jnp.exp(jax.random.uniform(k, (DEPTH, N_DELTA_HEADS), f32)
                     * (np.log(0.1) - np.log(0.001)) + np.log(0.001))
        return dt + jnp.log(-jnp.expm1(-dt))

    return {
        "x": jax.random.normal(ks[0], (BATCH, SEQ, D_MODEL), f32),
        "positions": jnp.broadcast_to(jnp.arange(SEQ, dtype=jnp.int32), (BATCH, SEQ)),
        "norm_mix_w": gain(ks[1], (DEPTH, D_MODEL)),
        "w_in": nrm(ks[2], (DEPTH, D_MODEL, PROJ_WIDTH), D_MODEL ** -0.5),
        "conv_qkv_w": nrm(ks[3], (DEPTH, SHORT_CONV_WIDTH, 3 * DELTA_WIDTH), SHORT_CONV_WIDTH ** -0.5),
        "a_log_fwd": jnp.log(jax.random.uniform(ks[4], (DEPTH, N_DELTA_HEADS), f32, 1.0, 16.0)),
        "a_log_bwd": jnp.log(jax.random.uniform(ks[5], (DEPTH, N_DELTA_HEADS), f32, 1.0, 16.0)),
        "dt_bias_fwd": dt_bias(ks[6]),
        "dt_bias_bwd": dt_bias(ks[7]),
        "delta_norm_w": gain(ks[8], (DEPTH, HEAD_DIM)),
        "w_out": nrm(ks[9], (DEPTH, MIX_WIDTH, D_MODEL), MIX_WIDTH ** -0.5),
        "norm_ffn_w": gain(ks[10], (DEPTH, D_MODEL)),
        "w_ffn_in": nrm(ks[11], (DEPTH, D_MODEL, 2 * D_FF), D_MODEL ** -0.5),
        "conv_ffn_w": nrm(ks[12], (DEPTH, FFN_CONV_WIDTH, 2 * D_FF), FFN_CONV_WIDTH ** -0.5),
        "w_ffn_out": nrm(ks[13], (DEPTH, D_FF, D_MODEL), D_FF ** -0.5),
        "norm_final_w": gain(ks[14], (D_MODEL,)),
    }

def first_block(x, positions, norm_mix_w, w_in, conv_qkv_w, a_log_fwd, a_log_bwd, dt_bias_fwd,
              dt_bias_bwd, delta_norm_w, w_out, norm_ffn_w, w_ffn_in, conv_ffn_w, w_ffn_out,
              norm_final_w):
    h = x
    for layer in range(DEPTH):
        n = rms_norm(h, norm_mix_w[layer])
        h = h + token_mixer(n, positions, w_in[layer], conv_qkv_w[layer], a_log_fwd[layer],
                            a_log_bwd[layer], dt_bias_fwd[layer], dt_bias_bwd[layer],
                            delta_norm_w[layer], w_out[layer]).astype(h.dtype)
        n = rms_norm(h, norm_ffn_w[layer])
        h = h + conv_gated_mlp(n, w_ffn_in[layer], conv_ffn_w[layer], w_ffn_out[layer]).astype(h.dtype)
    return rms_norm(h, norm_final_w)


CTX_LEN = 256
GRID_W = 64
W_BRANCH = D_MODEL // 2
NA_HEADS = 16
NA_HEAD_DIM = W_BRANCH // NA_HEADS
NA_WIN_H = 8
NA_WIN_W = 16
POOL_WINDOWS = (2, 4, 8, 16)
POOL_GROUPS = len(POOL_WINDOWS)
POOL_GROUP_DIM = W_BRANCH // POOL_GROUPS
RWKV_HEAD_DIM = 64
RWKV_HEADS = W_BRANCH // RWKV_HEAD_DIM
RWKV_LORA = 64
RMS_EPS = 1e-6
LNX_EPS = 64e-5
NEG_INF_2 = -1e30
IN_SIZES = (W_BRANCH,) * 10 + (RWKV_LORA, RWKV_LORA, N_BRANCH * D_MODEL)
IN_SPLIT_POINTS = tuple(int(s) for s in np.cumsum(IN_SIZES)[:-1])
D_IN = int(sum(IN_SIZES))


def rms_norm_2(x, g):
    xf = x.astype(jnp.float32)
    y = xf * lax.rsqrt(jnp.mean(xf * xf, axis=-1, keepdims=True) + RMS_EPS)
    return (y * g).astype(x.dtype)

def adaln_modulation(cond, w_mod, b_mod):
    m = jax.nn.silu(cond) @ w_mod + b_mod
    return jnp.split(m, 3, axis=-1)

def to_heads(z, n_heads):
    return z.reshape(z.shape[:-1] + (n_heads, z.shape[-1] // n_heads))

def neighbourhood_attention(q, k, v, k_ctx, v_ctx, rpb):
    B, T, H, Dh = q.shape
    rows = T // GRID_W
    win_h = min(NA_WIN_H, rows)
    scale = Dh ** -0.5
    qg = q.reshape(B, rows, GRID_W, H, Dh)
    kg = k.reshape(B, rows, GRID_W, H, Dh)
    vg = v.reshape(B, rows, GRID_W, H, Dh)
    col = jnp.arange(GRID_W)
    col_start = jnp.clip(col - NA_WIN_W // 2, 0, GRID_W - NA_WIN_W)
    col_mask = (col[None, :] >= col_start[:, None]) & (col[None, :] < col_start[:, None] + NA_WIN_W)
    col_off = jnp.clip(col[None, :] - col[:, None] + NA_WIN_W - 1, 0, 2 * NA_WIN_W - 2)
    n_loc = win_h * GRID_W

    def one_row(r):
        r0 = jnp.clip(r - win_h // 2, 0, rows - win_h)
        kb = lax.dynamic_slice_in_dim(kg, r0, win_h, axis=1)
        vb = lax.dynamic_slice_in_dim(vg, r0, win_h, axis=1)
        qr = lax.dynamic_index_in_dim(qg, r, axis=1, keepdims=False)
        row_off = r0 + jnp.arange(win_h) - r + NA_WIN_H - 1
        bias = jnp.take(jnp.take(rpb, row_off, axis=1), col_off, axis=2)
        bias = bias.transpose(0, 2, 1, 3).astype(jnp.float32)
        s_loc = jnp.einsum('bqhd,bkwhd->bhqkw', qr, kb, preferred_element_type=jnp.float32) * scale + bias[None]
        s_loc = jnp.where(col_mask[None, None, :, None, :], s_loc, NEG_INF_2)
        s_ctx = jnp.einsum('bqhd,bchd->bhqc', qr, k_ctx, preferred_element_type=jnp.float32) * scale
        s = jnp.concatenate([s_loc.reshape(B, H, GRID_W, n_loc), s_ctx], axis=-1)
        p = jax.nn.softmax(s, axis=-1).astype(v.dtype)
        p_loc = p[..., :n_loc].reshape(B, H, GRID_W, win_h, GRID_W)
        return (jnp.einsum('bhqkw,bkwhd->bqhd', p_loc, vb)
                + jnp.einsum('bhqc,bchd->bqhd', p[..., n_loc:], v_ctx))

    out = lax.map(one_row, jnp.arange(rows))
    return out.transpose(1, 0, 2, 3, 4).reshape(B, T, H * Dh)

def context_attention(q, k, v):
    s = jnp.einsum('bqhd,bkhd->bhqk', q, k, preferred_element_type=jnp.float32) * q.shape[-1] ** -0.5
    p = jax.nn.softmax(s, axis=-1).astype(v.dtype)
    o = jnp.einsum('bhqk,bkhd->bqhd', p, v)
    return o.reshape(o.shape[:2] + (-1,))

def multiscale_pool(u, pool_w, pool_scale):
    B, T, _ = u.shape
    uf = u.astype(jnp.float32).reshape(B, T, POOL_GROUPS, POOL_GROUP_DIM)
    csum = jnp.concatenate([jnp.zeros_like(uf[:, :1]), jnp.cumsum(uf, axis=1)], axis=1)
    t = jnp.arange(T)
    pooled = []
    for g, win in enumerate(POOL_WINDOWS):
        lo = jnp.maximum(t - win // 2, 0)
        hi = jnp.minimum(t + win // 2, T)
        cg = csum[:, :, g]
        pooled.append((cg[:, hi] - cg[:, lo]) / (hi - lo).astype(jnp.float32)[None, :, None])
    diff = (jnp.stack(pooled, axis=2) - uf).astype(u.dtype)
    y = jnp.einsum('btgc,gcd->btgd', diff, pool_w)
    return y.reshape(B, T, -1) * pool_scale

def centred_neighbour_mean(z):
    zp = jnp.pad(z, ((0, 0), (1, 1), (0, 0)))
    return 0.5 * (zp[:, :-2] + zp[:, 2:])

def rwkv_features(r0, k0, v0, lw, la, mu, w0, w2, a0, a2, k_k, k_a):
    f32 = jnp.float32
    r, k, v = (z + m * (centred_neighbour_mean(z) - z)
               for z, m in ((r0.astype(f32), mu[0]), (k0.astype(f32), mu[1]), (v0.astype(f32), mu[2])))
    kk = to_heads(k * k_k, RWKV_HEADS)
    kk = kk / jnp.maximum(jnp.sqrt(jnp.sum(kk * kk, axis=-1, keepdims=True)), 1e-12)
    lw_t = jnp.tanh(lw.astype(f32))
    la_f = la.astype(f32)
    dirs = []
    for d in range(2):
        w_log = -jax.nn.softplus(-(w0[d] + lw_t @ w2[d])) - 0.5
        decay = jnp.exp(-jnp.exp(w_log))
        a = jax.nn.sigmoid(a0[d] + la_f @ a2[d])
        k_d = k * (1 + (a - 1) * k_a)
        dirs.append((to_heads(decay, RWKV_HEADS), to_heads(k_d, RWKV_HEADS), -kk, kk * to_heads(a, RWKV_HEADS)))
    return to_heads(r, RWKV_HEADS), to_heads(v, RWKV_HEADS), dirs

def wkv_scan(r, v, decay, k, a_in, b_in, s0, reverse):
    def step(S, inp):
        rt, vt, wt, kt, at, bt = inp
        sa = jnp.einsum('bhij,bhj->bhi', S, at)
        S = S * wt[:, :, None, :] + sa[..., None] * bt[:, :, None, :] + vt[..., None] * kt[:, :, None, :]
        return S, jnp.einsum('bhij,bhj->bhi', S, rt)
    xs = tuple(jnp.moveaxis(z, 1, 0) for z in (r, v, decay, k, a_in, b_in))
    s_end, ys = lax.scan(step, s0, xs, reverse=reverse)
    return jnp.moveaxis(ys, 0, 1), s_end

def rwkv_readout(r, v, ys, dirs, r_k, g, b):
    y = ys[0] + ys[1]
    mu = jnp.mean(y, axis=-1, keepdims=True)
    var = jnp.mean(jnp.square(y - mu), axis=-1, keepdims=True)
    y = (y - mu) * lax.rsqrt(var + LNX_EPS) * to_heads(g, RWKV_HEADS) + to_heads(b, RWKV_HEADS)
    bonus = (jnp.sum(r * dirs[0][1] * r_k, axis=-1, keepdims=True)
             + jnp.sum(r * dirs[1][1] * r_k, axis=-1, keepdims=True)) * v
    out = y + bonus
    return out.reshape(out.shape[:2] + (-1,))

def hybrid_layer(x_lat, x_ctx, c, c_ctx, norm_g, w_mod, b_mod, w_in, na_rpb, pool_w, pool_scale,
                 rw_mu, rw_w0, rw_w2, rw_a0, rw_a2, rw_k_k, rw_k_a, rw_r_k, rw_lnx_g, rw_lnx_b,
                 w_branch, w_out, compute_ctx):
    n_ctx = x_ctx.shape[1]
    shift_l, scale_l, gate_l = adaln_modulation(c, w_mod, b_mod)
    shift_c, scale_c, gate_c = adaln_modulation(c_ctx, w_mod, b_mod)
    h_lat = rms_norm_2(x_lat, norm_g) * (1 + scale_l[:, None]) + shift_l[:, None]
    h_ctx = rms_norm_2(x_ctx, norm_g) * (1 + scale_c) + shift_c
    h = jnp.concatenate([h_ctx, h_lat], axis=1)
    (na_q, na_k, na_v, na_gate, pool_u, pool_gate, rw_r, rw_k, rw_v, rw_gate,
     rw_lw, rw_la, merge_logits) = jnp.split(h @ w_in, IN_SPLIT_POINTS, axis=-1)

    def cpart(z):
        return z[:, :n_ctx]

    def lpart(z):
        return z[:, n_ctx:]

    keep = (lambda z: z) if compute_ctx else lpart

    q, k, v = (to_heads(z, NA_HEADS) for z in (na_q, na_k, na_v))
    y_na = neighbourhood_attention(lpart(q), lpart(k), lpart(v), cpart(k), cpart(v), na_rpb)
    if compute_ctx:
        y_na = jnp.concatenate([context_attention(cpart(q), cpart(k), cpart(v)), y_na], axis=1)

    y_pool = multiscale_pool(lpart(pool_u), pool_w, pool_scale)
    if compute_ctx:
        y_pool = jnp.concatenate([multiscale_pool(cpart(pool_u), pool_w, pool_scale), y_pool], axis=1)

    rw_params = (rw_mu, rw_w0, rw_w2, rw_a0, rw_a2, rw_k_k, rw_k_a)
    r_c, v_c, dirs_c = rwkv_features(*(cpart(z) for z in (rw_r, rw_k, rw_v, rw_lw, rw_la)), *rw_params)
    r_l, v_l, dirs_l = rwkv_features(*(lpart(z) for z in (rw_r, rw_k, rw_v, rw_lw, rw_la)), *rw_params)
    ys_c, ys_l = [], []
    for d in range(2):
        s0 = jnp.zeros((h.shape[0], RWKV_HEADS, RWKV_HEAD_DIM, RWKV_HEAD_DIM), jnp.float32)
        y_c, s_ctx_end = wkv_scan(r_c, v_c, *dirs_c[d], s0, reverse=(d == 1))
        y_l, _ = wkv_scan(r_l, v_l, *dirs_l[d], s_ctx_end, reverse=(d == 1))
        ys_c.append(y_c)
        ys_l.append(y_l)
    y_rw = rwkv_readout(r_l, v_l, ys_l, dirs_l, rw_r_k, rw_lnx_g, rw_lnx_b)
    if compute_ctx:
        y_rw = jnp.concatenate([rwkv_readout(r_c, v_c, ys_c, dirs_c, rw_r_k, rw_lnx_g, rw_lnx_b), y_rw], axis=1)

    dt = h.dtype
    b_na = y_na.astype(dt) * jax.nn.silu(keep(na_gate))
    b_pool = y_pool.astype(dt) * jax.nn.silu(keep(pool_gate))
    b_rw = y_rw.astype(dt) * jax.nn.silu(keep(rw_gate))
    g_na, g_pool, g_rw = jnp.split(jax.nn.sigmoid(keep(merge_logits)), N_BRANCH, axis=-1)
    merged = g_na * (b_na @ w_branch[0]) + g_pool * (b_pool @ w_branch[1]) + g_rw * (b_rw @ w_branch[2])
    out = merged @ w_out
    if compute_ctx:
        return x_lat + gate_l[:, None] * lpart(out), x_ctx + gate_c * cpart(out)
    return x_lat + gate_l[:, None] * out, None

def second_inputs(seed: int = 0) -> dict:
    key = jax.random.key(seed)
    ks = jax.random.split(key, 24)
    f32 = jnp.float32
    D, L, W, R = D_MODEL, DEPTH, W_BRANCH, RWKV_LORA

    def nrm(k, shape, std):
        return jax.random.normal(k, shape, f32) * std

    return {
        "x": nrm(ks[0], (BATCH, SEQ, D), 1.0),
        "c": nrm(ks[1], (BATCH, D), 1.0),
        "ctx": nrm(ks[2], (BATCH, CTX_LEN, D), 1.0),
        "c_ctx": nrm(ks[3], (D,), 1.0),
        "norm_g": 1.0 + nrm(ks[4], (L, D), 0.05),
        "w_mod": nrm(ks[5], (L, D, 3 * D), 0.5 * D ** -0.5),
        "b_mod": nrm(ks[6], (L, 3 * D), 0.02),
        "w_in": nrm(ks[7], (L, D, D_IN), D ** -0.5),
        "na_rpb": nrm(ks[8], (L, NA_HEADS, 2 * NA_WIN_H - 1, 2 * NA_WIN_W - 1), 0.1),
        "pool_w": nrm(ks[9], (L, POOL_GROUPS, POOL_GROUP_DIM, POOL_GROUP_DIM), POOL_GROUP_DIM ** -0.5),
        "pool_scale": 1.0 + nrm(ks[10], (L, W), 0.1),
        "rw_mu": jax.random.uniform(ks[11], (L, 3, W), f32),
        "rw_w0": jax.random.uniform(ks[12], (L, 2, W), f32, -6.0, -1.0),
        "rw_w2": nrm(ks[13], (L, 2, R, W), 0.5 * R ** -0.5),
        "rw_a0": nrm(ks[14], (L, 2, W), 0.5),
        "rw_a2": nrm(ks[15], (L, 2, R, W), 0.5 * R ** -0.5),
        "rw_k_k": 0.85 + nrm(ks[16], (L, W), 0.05),
        "rw_k_a": 1.0 + nrm(ks[17], (L, W), 0.05),
        "rw_r_k": nrm(ks[18], (L, RWKV_HEADS, RWKV_HEAD_DIM), 0.1),
        "rw_lnx_g": 1.0 + nrm(ks[19], (L, W), 0.05),
        "rw_lnx_b": nrm(ks[20], (L, W), 0.02),
        "w_branch": nrm(ks[21], (L, N_BRANCH, W, D), W ** -0.5),
        "w_out": nrm(ks[22], (L, D, D), D ** -0.5),
        "final_g": 1.0 + nrm(ks[23], (D,), 0.05),
    }

def second_block(x, c, ctx, c_ctx, norm_g, w_mod, b_mod, w_in, na_rpb, pool_w, pool_scale,
              rw_mu, rw_w0, rw_w2, rw_a0, rw_a2, rw_k_k, rw_k_a, rw_r_k, rw_lnx_g, rw_lnx_b,
              w_branch, w_out, final_g):
    x_lat, x_ctx = x, ctx
    for layer in range(DEPTH):
        x_lat, x_ctx = hybrid_layer(
            x_lat, x_ctx, c, c_ctx, norm_g[layer], w_mod[layer], b_mod[layer], w_in[layer],
            na_rpb[layer], pool_w[layer], pool_scale[layer], rw_mu[layer], rw_w0[layer], rw_w2[layer],
            rw_a0[layer], rw_a2[layer], rw_k_k[layer], rw_k_a[layer], rw_r_k[layer], rw_lnx_g[layer],
            rw_lnx_b[layer], w_branch[layer], w_out[layer], compute_ctx=(layer < DEPTH - 1))
    return rms_norm_2(x_lat, final_g)


def setup_inputs(seed=0):
    out = dict(first_inputs(seed))
    for name, value in second_inputs(seed + 1).items():
        if name != "x":
            out[name + "_2"] = value
    return out


def reference(
    x, positions, norm_mix_w, w_in, conv_qkv_w, a_log_fwd, a_log_bwd, dt_bias_fwd, dt_bias_bwd,
    delta_norm_w, w_out, norm_ffn_w, w_ffn_in, conv_ffn_w, w_ffn_out, norm_final_w, c_2, ctx_2,
    c_ctx_2, norm_g_2, w_mod_2, b_mod_2, w_in_2, na_rpb_2, pool_w_2, pool_scale_2, rw_mu_2,
    rw_w0_2, rw_w2_2, rw_a0_2, rw_a2_2, rw_k_k_2, rw_k_a_2, rw_r_k_2, rw_lnx_g_2, rw_lnx_b_2,
    w_branch_2, w_out_2, final_g_2,
):
    x = first_block(
        x, positions, norm_mix_w, w_in, conv_qkv_w, a_log_fwd, a_log_bwd, dt_bias_fwd,
        dt_bias_bwd, delta_norm_w, w_out, norm_ffn_w, w_ffn_in, conv_ffn_w, w_ffn_out,
        norm_final_w,
    )
    return second_block(
        x, c_2, ctx_2, c_ctx_2, norm_g_2, w_mod_2, b_mod_2, w_in_2, na_rpb_2, pool_w_2,
        pool_scale_2, rw_mu_2, rw_w0_2, rw_w2_2, rw_a0_2, rw_a2_2, rw_k_k_2, rw_k_a_2, rw_r_k_2,
        rw_lnx_g_2, rw_lnx_b_2, w_branch_2, w_out_2, final_g_2,
    )


_drawn_inputs = setup_inputs


def setup_inputs(seed=0):
    import zlib

    import numpy as np

    out = dict(_drawn_inputs(seed))
    spreads = {}
    factors = {'norm_mix_w': 3.861,
     'delta_norm_w': 6.03,
     'norm_ffn_w': 3.936,
     'norm_final_w': 2.72,
     'norm_g_2': 3.874,
     'b_mod_2': 3.989,
     'na_rpb_2': 200.0,
     'pool_scale_2': 17.894,
     'rw_w2_2': 8.0,
     'rw_k_k_2': 38.0,
     'rw_k_a_2': 4.713,
     'rw_lnx_g_2': 64.0,
     'rw_lnx_b_2': 200.0}
    for name, (base, spread) in spreads.items():
        noise = np.random.default_rng([zlib.crc32(name.encode()), seed]).standard_normal(out[name].shape)
        drawn = base * np.exp(spread * noise) if base else spread * noise
        out[name] = jnp.asarray(drawn.astype(out[name].dtype))
    for name, factor in factors.items():
        out[name] = (out[name] * factor).astype(out[name].dtype)
    return out
```

```python
import concourse.bass as bass
from concourse import mybir
import numpy as np

F32 = mybir.dt.float32
FR = mybir.dt.float32r
I32 = mybir.dt.int32
ACT = mybir.ActivationFunctionType
ALU = mybir.AluOpType
AX = mybir.AxisListType

P = 128
D = 2048
KT = D // P
T = 256
TT = T // P
HEADS = 8
DFF = 5632
FT = DFF // P
CHUNK = 64
EPS = 1e-6
NEG = -1e30
NBR = 3
QSCALE = float(P) ** -0.5
GRID, WIN = 64, 16
DECAY = -float(np.exp(-0.5))
LNX_EPS = 64e-5
WT = 8


class Chain:

    def __init__(self, eng, sem):
        self.eng, self.sem, self.n, self.it, self.per = eng, sem, 0, None, 0

    def enter(self, it, per):
        self.it, self.per, self.base = it, per, self.n

    def leave(self, trips):
        assert self.n - self.base == self.per, (self.sem, "per iteration", self.n - self.base)
        self.n = self.base + self.per * trips
        self.it = None

    def __call__(self, ins):
        self.n += 1
        ins.then_inc(self.sem, 1)
        self.eng.wait_ge(self.sem, self.n if self.it is None else self.it * self.per + self.n)


def at(p, add=0, div=1, mul=1):
    k, it, per = p
    v = (k // div + add) * mul
    return v if it is None else it * (per // div * mul) + v


def constants():
    s, t = np.arange(P)[:, None], np.arange(P)[None, :]
    same = lambda n: s // n == t // n
    c = {}
    c["ones"] = np.ones((P, P))
    c["ident"] = np.eye(P)
    c["pairs"] = same(CHUNK)
    c["upto"] = np.concatenate([same(CHUNK) & (s <= t), same(CHUNK) & (s >= t)], 1)
    c["before"] = np.concatenate([same(CHUNK) & (s < t), same(CHUNK) & (s > t)], 1)
    c["chunk"] = np.concatenate([(s < CHUNK) & (t >= 0), (s >= CHUNK) & (t >= 0)], 1)
    c["block8"] = same(8)
    c["merge"] = np.concatenate([same(2 * n) & ~same(n) for n in (8, 16, 32)], 1)
    turn = np.zeros((P, 64))
    for m in range(16):
        turn[m + 16, m] = -1.0
        turn[m, m + 16] = 1.0
    c["turn"] = turn
    start = np.ones((P, P))
    start[:, ::CHUNK] = 0.0
    c["carry"] = start
    inv = (500000.0 ** (-np.arange(0, 32, 2, dtype=np.float32) / np.float32(32))).astype(np.float32)
    f = np.zeros((P, 1), np.float32)
    f[:32, 0] = np.concatenate([inv, inv])
    c["freq"] = f
    c["eps"] = np.full((P, 1), EPS)
    c["zero"] = np.zeros((P, 1))
    return c


def const_columns():
    at_, out = 0, {}
    for name, a in constants().items():
        out[name] = (at_, a.shape[1])
        at_ += a.shape[1]
    return out, at_


def near_columns():
    c = np.arange(GRID)
    start = np.clip(c - WIN // 2, 0, GRID - WIN)
    ok = (c[None, :] >= start[:, None]) & (c[None, :] < start[:, None] + WIN)
    return np.tile(np.where(ok, 0.0, NEG).astype(np.float32), (2, 1))


def pool_matrices():
    s, t = np.arange(T)[:, None], np.arange(T)[None, :]
    out = np.zeros((T, 4, T), np.float32)
    for g, win in enumerate((2, 4, 8, 16)):
        lo, hi = np.maximum(t - win // 2, 0), np.minimum(t + win // 2, T)
        out[:, g] = ((s >= lo) & (s < hi)) / (hi - lo).astype(np.float32) - (s == t)
    return out.reshape(TT, P, 4, T).transpose(1, 2, 0, 3)


def dilated_masks():
    q = np.arange(T)[:, None]
    k = np.arange(T)[None, :]
    out = np.zeros((P, TT, NBR, T), np.float32)
    for b, (window, dil) in enumerate(((128, 1), (512, 4), (2048, 16))):
        half = window // (2 * dil)
        ok = ((q - k) % dil == 0) & (np.abs(q - k) <= half * dil)
        m = np.where(ok, 0.0, NEG).reshape(TT, P, T)
        out[:, :, b] = m.transpose(1, 0, 2)
    return out


def program(nc, a, out):
    base = -(-nc.sbuf_base // 64) * 64
    sems, mem = {}, {}

    def S(name):
        if name not in sems:
            sems[name] = nc.alloc_semaphore(name)
        return sems[name]

    def place(name, kb, shape, dtype=F32):
        mem[name] = nc.alloc_sbuf_tensor_at(name, shape, dtype, offset=base + int(kb * 1024))
        return mem[name]

    cc, ncc = const_columns()
    ring = place("ring", 0, [P, 2, KT * P])
    w_hi = place("w_hi", 16, [P, 2, KT * P], FR)
    w_lo = place("w_lo", 32, [P, 2, KT * P], FR)
    x_hi = place("x_hi", 48, [P, KT, T], FR)
    x_lo = place("x_lo", 64, [P, KT, T], FR)
    consts = place("consts", 80, [P, ncc])
    small = place("small", 87.3125, [P, 1100])
    C = lambda name, j=0, n=P: consts[:, cc[name][0] + j * n:cc[name][0] + (j + 1) * n]
    one = lambda name: consts[:, cc[name][0]:cc[name][0] + 1]
    EPSC, ZERO = one("eps"), one("zero")

    def smalls(at_, n):
        return small[:, at_:at_ + n]

    g_mix, g_ffn, g_fin = smalls(0, 16), smalls(16, 16), smalls(32, 16)
    cw_qkv = smalls(48, 120)
    alog, dtb = smalls(168, 16), smalls(184, 16)
    dnorm = smalls(200, 1)
    cw_ffn = smalls(201, 264)
    CUR = 470
    gates_f = small[:, CUR:CUR + 32].rearrange("p (t c) -> p t c", t=TT)
    beta = small[:, CUR + 32:CUR + 64].rearrange("p (t c) -> p t c", t=TT)
    gtmp = small[:, CUR + 64:CUR + 96].rearrange("p (t c) -> p t c", t=TT)
    gcur = small[:, CUR + 96:CUR + 112].rearrange("p (t d j) -> p t d j", t=TT, d=2)
    bcur = small[:, CUR + 112:CUR + 128].rearrange("p (t d j) -> p t d j", t=TT, d=2)
    nbcur = small[:, CUR + 128:CUR + 144].rearrange("p (t d j) -> p t d j", t=TT, d=2)
    sums = small[:, CUR + 144:CUR + 208].rearrange("p (k t d j) -> p k t d j", k=4, t=TT, d=2)
    esum = small[:, CUR + 208:CUR + 272].rearrange("p (k t d j) -> p k t d j", k=4, t=TT, d=2)
    necum = small[:, CUR + 272:CUR + 288].rearrange("p (t d j) -> p t d j", t=TT, d=2)
    stat = small[:, CUR + 290:CUR + 320]

    W0 = 92
    x = place("x", W0, [P, KT, T])
    mixed = place("mixed", W0 + 16, [P, KT, T])
    D0 = W0 + 32
    raw = place("raw", D0, [P, 12, T + 4])
    Sv = place("Sv", D0, [P, 3, 2, 4, P])
    qkv = place("qkv", D0 + 12.25, [P, 12, T])
    Oacc = place("Oacc", D0 + 12.25 + 8, [P, 4, T])
    zg = place("zg", D0 + 24.25, [P, 4, T])
    vtok = place("vtok", D0 + 28.25, [P, TT, 4, P])
    ktok = place("ktok", D0 + 32.25, [P, TT, 4, P])
    qdec = place("qdec", D0 + 36.25, [P, 2, 4, P])
    QKT = place("QKT", D0 + 40.25, [P, 2, 4, P])
    I0 = D0 + 44.25
    inv = lambda name, k: place(name, I0 + 4 * k, [P, 2, 4, P])
    NT, N_, A_, AT = inv("NT", 0), inv("N_", 1), inv("A_", 2), inv("AT", 3)
    B2, B2T, A4, XT, M_ = inv("B2", 4), inv("B2T", 5), inv("A4", 6), inv("XT", 7), inv("M_", 8)
    gam = inv("gam", 2)
    Rr, Vn, Kt = inv("Rr", 4), inv("Vn", 5), inv("Kt", 6)
    sq = place("sq", I0, [P, KT, T])

    dinv = (NT, N_, A_, AT, B2, B2T, A4, XT, M_)
    banks = [nc.alloc_psum_tensor(f"bank{i}", [P, 512], F32) for i in range(8)]
    b4 = lambda i: banks[i][:, :].rearrange("p (m c) -> p m c", m=4)

    plan = [("gates", 1, 1), ("delta", 16, 2), ("dil", 18, 4), ("wout", 2, 8), ("up", 4, 22), ("down", 22, 2),
            ("na", 8, 4), ("pool", 4, 4), ("lora", 1, 1), ("kv", 2, 8), ("rg", 2, 8),
            ("merge", 18, 4), ("wout2", 2, 8)]
    first, n = {}, 0
    for name, per, trips in plan:
        first[name] = n
        n += per * trips
    total = n

    def act_split(act, p, w=KT * P):
        s = p[0] % 2
        act.wait_ge(S(f"panel_loaded{s}"), at(p, 1, 2, 16))
        act.wait_ge(S("panel_used"), at(p, 1))
        nc.scalar.copy(w_hi[:, s, 0:w], ring[:, s, 0:w]).then_inc(S("panel_hi"), 1)

    def dve_split(dve, p, w=KT * P):
        s = p[0] % 2
        dve.wait_ge(S("panel_hi"), at(p, 1))
        nc.vector.tensor_tensor(w_lo[:, s, 0:w], ring[:, s, 0:w], w_hi[:, s, 0:w].bitcast(F32),
                                ALU.subtract).then_inc(S("panel_split"), 1)

    def ahead(p, k=2):
        return (p[0] + k, p[1], p[2])

    def tick(eng, split, p, w=KT * P):
        split(eng, ahead(p), w)

    def project(pe, p, rhs, out_ap, tiles=KT):
        s = p[0] % 2
        pe.wait_ge(S("panel_split"), at(p, 3))
        pe.wait_ge(S("proj_read"), at(p, 1))
        for k in range(tiles):
            hi, lo = w_hi[:, s, k * P:(k + 1) * P], w_lo[:, s, k * P:(k + 1) * P]
            xh, xl = rhs(k)
            nc.tensor.matmul(out_ap, hi, xh, start=k == 0, stop=False)
            nc.tensor.matmul(out_ap, hi, xl, start=False, stop=False)
            last = nc.tensor.matmul(out_ap, lo, xh, start=False, stop=k == tiles - 1)
        last.then_inc(S("panel_used"), 1)

    def project2(pe, p, rhs, bank):
        s = p[0] % 2
        pe.wait_ge(S("panel_split"), at(p, 3))
        pe.wait_ge(S("proj_read"), at(p, 1))
        for k in range(KT):
            hi, lo = w_hi[:, s, k * P:(k + 1) * P], w_lo[:, s, k * P:(k + 1) * P]
            for w, half in ((hi, 0), (hi, 1), (lo, 0)):
                for g in range(2):
                    last = nc.tensor.matmul(bank[:, g * T:(g + 1) * T], w, rhs(g, k)[half],
                                            start=k == 0 and g == 0 and w is hi and half == 0,
                                            stop=k == KT - 1 and w is lo and g == 1, skip_group_check=True)
        last.then_inc(S("panel_used"), 1)

    rhs_x = lambda k: (x_hi[:, k, :], x_lo[:, k, :])
    pbank = lambda p, n=T: banks[6 + p[0] % 2][:, 0:n]

    bars = {}

    def barrier(eng):
        bars[id(eng)] = bars.get(id(eng), 0) + 1
        eng.drain().then_inc(S("phase_done"), 1)
        eng.wait_ge(S("phase_done"), 4 * bars[id(eng)])

    for i in range(2):
        S(f"panel_loaded{i}")


    def norm_pe(pe, c):
        pe.wait_ge(S("sq_ready"), c)
        for k in range(KT):
            last = nc.tensor.matmul(banks[0][:, 0:T], C("ones"), sq[:, k, :], start=k == 0, stop=k == KT - 1)
        last.then_inc(S("ss_ready"), 1)

    def norm_act(act, c, src):
        nc.scalar.activation(sq[:, :, :], src, ACT.Square).then_inc(S("sq_ready"), 1)
        act.wait_ge(S("var_ready"), c)
        nc.scalar.activation(rstd, rstd, ACT.Sqrt).then_inc(S("std_ready"), 1)

    rstd = mixed[:, 0, :]

    def norm_dve(dve, ch, c, src, dst):
        dve.wait_ge(S("ss_ready"), c)
        nc.vector.tensor_scalar(rstd, banks[0][:, 0:T], 1.0 / D, EPS, ALU.mult, ALU.add).then_inc(S("var_ready"), 1)
        dve.wait_ge(S("std_ready"), c)
        ch(nc.vector.reciprocal(rstd, rstd))
        nc.vector.tensor_tensor(dst, src, rstd.rearrange("p (a t) -> p a t", a=1).to_broadcast([P, KT, T]),
                                ALU.mult).then_inc(S("normed"), 1)

    def gain_act(act, c, src, gain):
        act.wait_ge(S("normed"), c)
        for k in range(KT):
            nc.scalar.activation(x_hi[:, k, :], src[:, k, :], ACT.Copy, scale=gain[:, k:k + 1]).then_inc(S("xhi_ready"), 1)

    def gain_dve(dve, ch, c, src, gain):
        for k in range(KT):
            dve.wait_ge(S("xhi_ready"), (c - 1) * KT + k + 1)
            last = nc.vector.scalar_tensor_tensor(x_lo[:, k, :], src[:, k, :], gain[:, k:k + 1],
                                                  x_hi[:, k, :].bitcast(F32), ALU.mult, ALU.subtract)
        last.then_inc(S("xsplit"), 1)

    STEPS = 20

    def step(sg, k):
        return at((sg[0] * STEPS + k, sg[1], sg[2] * STEPS))

    def inv8(sg, k):
        return at((sg[0] * 8 + k, sg[1], sg[2] * 8))

    def inv10(sg, k):
        return at((sg[0] * 18 + k, sg[1], sg[2] * 18))

    def inv12(sg, k):
        return at((sg[0] * 12 + k, sg[1], sg[2] * 12))

    def bc(ap, m=4):
        return ap.rearrange("p (a c) -> p a c", a=1).to_broadcast([P, m, P])

    def inv_pe(pe, sg, buf):
        NT, N_, A_, AT, B2, B2T, A4, XT, M_ = buf
        for h in range(2):
            pe.wait_ge(S("nt_ready"), at((sg[0] * 2 + h, sg[1], sg[2] * 2), 1))
            for m in range(4):
                last = nc.tensor.transpose(b4(h)[:, m, :], NT[:, h, m, :], C("ident"))
            last.then_inc(S("inv_pe"), 1)
        for h in range(2):
            pe.wait_ge(S("inv_pool"), inv8(sg, 1 + h))
            pe.wait_ge(S("inv_dve"), inv10(sg, 1 + h))
            for m in range(4):
                nc.tensor.matmul(b4(h)[:, m, :], AT[:, h, m, :], A_[:, h, m, :], start=True, stop=True)
                last = nc.tensor.matmul(b4(2 + h)[:, m, :], A_[:, h, m, :], AT[:, h, m, :], start=True, stop=True)
            last.then_inc(S("inv_pe"), 1)
        for h in range(2):
            pe.wait_ge(S("inv_act"), inv12(sg, 3 + h))
            pe.wait_ge(S("inv_dve"), inv10(sg, 3 + h))
            for m in range(4):
                nc.tensor.matmul(b4(h)[:, m, :], B2[:, h, m, :], XT[:, h, m, :], start=True, stop=True)
                last = nc.tensor.matmul(b4(2 + h)[:, m, :], B2T[:, h, m, :], B2[:, h, m, :], start=True, stop=True)
            last.then_inc(S("inv_pe"), 1)
        for h in range(2):
            pe.wait_ge(S("inv_act"), inv12(sg, 5 + h))
            pe.wait_ge(S("inv_dve"), inv10(sg, 5 + h))
            for m in range(4):
                last = nc.tensor.matmul(b4(h)[:, m, :], A4[:, h, m, :], XT[:, h, m, :], start=True, stop=True)
            last.then_inc(S("inv_pe"), 1)
        for l in range(3):
            for h in range(2):
                pe.wait_ge(S("inv_dve"), inv10(sg, 7 + 4 * l + h))
                pe.wait_ge(S("inv_pool"), inv8(sg, 3 + 2 * l + h))
                for m in range(4):
                    nc.tensor.matmul(b4(h)[:, m, :], M_[:, h, m, :], XT[:, h, m, :], start=True, stop=True)
                    last = nc.tensor.transpose(b4(2 + h)[:, m, :], XT[:, h, m, :], C("ident"))
                last.then_inc(S("inv_pe"), 1)
            for h in range(2):
                pe.wait_ge(S("inv_dve"), inv10(sg, 9 + 4 * l + h))
                pe.wait_ge(S("inv_act"), inv12(sg, 7 + 2 * l + h))
                for m in range(4):
                    last = nc.tensor.matmul(b4(h)[:, m, :], A_[:, h, m, :], AT[:, h, m, :], start=True, stop=True)
                last.then_inc(S("inv_pe"), 1)

    def inv_act(act, sg, buf):
        NT, N_, A_, AT, B2, B2T, A4, XT, M_ = buf
        for h in range(2):
            act.wait_ge(S("inv_pe"), step(sg, 1 + h))
            nc.scalar.copy(N_[:, h], b4(h)).then_inc(S("inv_act"), 1)
        for h in range(2):
            act.wait_ge(S("inv_pe"), step(sg, 3 + h))
            nc.scalar.copy(B2[:, h], b4(h)).then_inc(S("inv_act"), 1)
        for h in range(2):
            act.wait_ge(S("inv_pe"), step(sg, 5 + h))
            nc.scalar.copy(A4[:, h], b4(2 + h)).then_inc(S("inv_act"), 1)
        for l in range(3):
            for h in range(2):
                act.wait_ge(S("inv_pe"), step(sg, 9 + 4 * l + h))
                nc.scalar.copy(A_[:, h], b4(2 + h)).then_inc(S("inv_act"), 1)

    def inv_dve(dve, ch, sg, buf):
        NT, N_, A_, AT, B2, B2T, A4, XT, M_ = buf
        for h in range(2):
            dve.wait_ge(S("nt_ready"), at((sg[0] * 2 + h, sg[1], sg[2] * 2), 1))
            ch(nc.vector.tensor_tensor(AT[:, h], NT[:, h], bc(C("block8")), ALU.mult))
            nc.vector.tensor_tensor(XT[:, h], AT[:, h], bc(C("ident")), ALU.add).then_inc(S("inv_dve"), 1)
        for h in range(2):
            dve.wait_ge(S("inv_pe"), step(sg, 3 + h))
            nc.vector.tensor_copy(B2T[:, h], b4(2 + h)).then_inc(S("inv_dve"), 1)
        for h in range(2):
            dve.wait_ge(S("inv_pe"), step(sg, 5 + h))
            nc.vector.tensor_tensor(XT[:, h], b4(h), XT[:, h], ALU.add).then_inc(S("inv_dve"), 1)
        for h in range(2):
            dve.wait_ge(S("inv_pe"), step(sg, 7 + h))
            nc.vector.tensor_tensor(XT[:, h], b4(h), XT[:, h], ALU.add).then_inc(S("inv_dve"), 1)
        for l in range(3):
            for h in range(2):
                dve.wait_ge(S("inv_pe"), step(sg, 9 + 4 * l + h))
                nc.vector.tensor_copy(AT[:, h], b4(h)).then_inc(S("inv_dve"), 1)
            for h in range(2):
                dve.wait_ge(S("inv_pe"), step(sg, 11 + 4 * l + h))
                last = nc.vector.tensor_tensor(XT[:, h], b4(h), XT[:, h], ALU.add)
                if l < 2:
                    last.then_inc(S("inv_dve"), 1)
                else:
                    last.then_inc(S("xt_ready"), 1)

    def inv_pool(pool, sg, buf):
        NT, N_, A_, AT, B2, B2T, A4, XT, M_ = buf
        for h in range(2):
            pool.wait_ge(S("inv_act"), inv12(sg, 1 + h))
            nc.gpsimd.tensor_tensor(A_[:, h], N_[:, h], bc(C("block8")), ALU.mult).then_inc(S("inv_pool"), 1)
        for l in range(3):
            for h in range(2):
                if l:
                    pool.wait_ge(S("inv_pe"), step(sg, 5 + 4 * l + h))
                nc.gpsimd.tensor_tensor(M_[:, h], N_[:, h], bc(C("merge", l)), ALU.mult).then_inc(S("inv_pool"), 1)

    def load_first(pool):
        pool.dma_start(consts[:, :], a["consts"]).then_inc(S("loaded0"), 16)
        pool.dma_start(small[:, 0:CUR], a["small"]).then_inc(S("loaded0"), 16)

    def gates_pe(pe):
        p = (first["gates"], None, 0)
        project(pe, p, rhs_x, pbank(p))
        pe.wait_ge(S("gate_rows"), 1)
        for t in range(TT):
            last = nc.tensor.transpose(banks[0][:, t * P:(t + 1) * P], qkv[:, 0, t * P:(t + 1) * P], C("ident"))
        last.then_inc(S("gate_cols"), 1)

    def gates_act(act):
        p = (first["gates"], None, 0)
        act.wait_ge(S("panel_used"), at(p, 3))
        nc.scalar.copy(qkv[:, 0, :], pbank(p)).then_inc(S("gate_rows"), 1)
        act.wait_ge(S("gate_rows"), 1)
        act.sem_inc(S("proj_read"), 1)
        tick(act, act_split, p)
        act.wait_ge(S("gate_abs"), 1)
        nc.scalar.activation(gtmp[:, :, 0:16], gtmp[:, :, 0:16], ACT.Exp).then_inc(S("gate_e"), 1)
        act.wait_ge(S("gate_e"), 1)
        nc.scalar.activation(gtmp[:, :, 0:16], gtmp[:, :, 0:16], ACT.Ln, bias=1.0).then_inc(S("gate_e"), 1)
        nc.scalar.activation(alog, alog, ACT.Exp).then_inc(S("gate_e"), 1)
        nc.scalar.activation(beta[:, :, 0:16], banks[0][:, 0:TT * P].rearrange("p (t c) -> p t c", t=TT)[:, :, 16:32],
                             ACT.Sigmoid).then_inc(S("gate_e"), 1)

    def gates_dve(dve, ch):
        p = (first["gates"], None, 0)
        tick(dve, dve_split, p)
        dve.wait_ge(S("gate_cols"), 1)
        cols = banks[0][:, 0:TT * P].rearrange("p (t c) -> p t c", t=TT)
        dt_b = dtb.rearrange("p (a c) -> p a c", a=1).to_broadcast([P, TT, 16])
        ga = gates_f[:, :, 0:16]
        ch(nc.vector.tensor_tensor(ga, cols[:, :, 0:16], dt_b, ALU.add))
        ch(nc.vector.tensor_scalar(gtmp[:, :, 0:16], ga, -1.0, None, ALU.mult))
        nc.vector.tensor_tensor(gtmp[:, :, 0:16], gtmp[:, :, 0:16], ga, ALU.min).then_inc(S("gate_abs"), 1)
        ch(nc.vector.tensor_scalar(ga, ga, 0.0, None, ALU.max))
        dve.wait_ge(S("gate_e"), 4)
        ch(nc.vector.tensor_tensor(ga, ga, gtmp[:, :, 0:16], ALU.add))
        al = alog.rearrange("p (a c) -> p a c", a=1).to_broadcast([P, TT, 16])
        ch(nc.vector.scalar_tensor_tensor(ga, ga, -1.0, al, ALU.mult, ALU.mult))

    def delta_tile(d, tau):
        return tau if d == 0 else 1 - tau

    def delta_pe(pe, it):
        for k in range(16):
            p = (first["delta"] + k, it, 16)
            project(pe, p, rhs_x, pbank(p))
        n1 = lambda k, per: at((k, it, per))
        pe.wait_ge(S("qk_sq"), n1(1, 1))
        for b in range(4):
            last = nc.tensor.matmul(banks[b][:, :], C("ones"), sq[:, 2 * b:2 * b + 2, :], start=True, stop=True)
        last.then_inc(S("qk_ss"), 1)
        pe.wait_ge(S("qk_normed"), n1(1, 1))
        for j in range(4):
            for t in range(TT):
                nc.tensor.transpose(b4(t)[:, j, :], qkv[:, 8 + j, t * P:(t + 1) * P], C("ident"))
                last = nc.tensor.transpose(b4(2 + t)[:, j, :], qkv[:, 4 + j, t * P:(t + 1) * P], C("ident"))
        last.then_inc(S("kv_turned"), 1)
        pe.wait_ge(S("gcur_ready"), n1(1, 1))
        for t in range(TT):
            for d in range(2):
                g = gcur[:, t, d, :]
                for k, m in enumerate((C("upto", d), C("before", 1 - d), C("chunk", 0), C("chunk", 1))):
                    o = ((k * 2 + t) * 2 + d) * 4
                    last = nc.tensor.matmul(banks[4][:, o:o + 4], m, g, start=True, stop=True)
        last.then_inc(S("sums_ready"), 1)
        pe.wait_ge(S("esum_ready"), n1(1, 1))
        pe.wait_ge(S("delta_ready"), n1(2, 2))
        for tau in range(2):
            sg = (tau, it, 2)
            n2 = lambda k, per=1: at((tau * per + k, it, 2 * per))
            if tau:
                pe.wait_ge(S("o_read"), n2(0, 2))
            for d in range(2):
                ts = delta_tile(d, tau) * P
                for j in range(4):
                    nc.tensor.matmul(b4(d)[:, j, :], gcur[:, ts // P, d, j:j + 1].to_broadcast([P, P]),
                                     C("upto", d), start=True, stop=True)
                    kk = qkv[:, 4 + j, ts:ts + P]
                    nc.tensor.matmul(b4(2 + d)[:, j, :], kk, kk, start=True, stop=True)
                    last = nc.tensor.matmul(b4(4 + d)[:, j, :], kk, qkv[:, j, ts:ts + P], start=True, stop=True)
                last.then_inc(S("pairs_ready"), 1)
            inv_pe(pe, (tau, it, 2), dinv)
            for c in range(2):
                m = lambda k, per: at(((tau * 2 + c) * per + k, it, 4 * per))
                for d in range(2):
                    ts = delta_tile(d, tau) * P
                    if c == 0:
                        pe.wait_ge(S("xt_ready"), n2(d + 1, 2))
                    pe.wait_ge(S("state_ready"), at((tau * 4 + c * 2 + d + 1, it, 8)))
                    for j in range(4):
                        last = nc.tensor.matmul(b4(d)[:, j, :], qkv[:, 4 + j, ts:ts + P], state(tau, c)[:, d, j, :],
                                                start=True, stop=True)
                    last.then_inc(S("ks_ready"), 1)
                for d in range(2):
                    pe.wait_ge(S("r_ready"), m(d + 1, 2))
                    for j in range(4):
                        last = nc.tensor.matmul(b4(2 + d)[:, j, :], XT[:, d, j, :], Rr[:, d, j, :], start=True, stop=True)
                    last.then_inc(S("w_ready"), 1)
                for d in range(2):
                    r0 = CHUNK * (c if d == 0 else 1 - c)
                    pe.wait_ge(S("vnew_ready"), m(d + 1, 2))
                    for j in range(4):
                        last = nc.tensor.matmul(b4(4 + d)[:, j, :], Kt[r0:r0 + CHUNK, d, j, :],
                                                Vn[r0:r0 + CHUNK, d, j, :], start=True, stop=True)
                    last.then_inc(S("ds_ready"), 1)
            for d in range(2):
                pe.wait_ge(S("qdec_ready"), n2(d + 1, 2))
                pe.wait_ge(S("qkt_ready"), n2(d + 1, 2))
                for j in range(4):
                    for c in range(2):
                        r0 = CHUNK * (c if d == 0 else 1 - c)
                        nc.tensor.matmul(b4(d)[:, j, r0:r0 + CHUNK], state(tau, c)[:, d, j, :],
                                         qdec[:, d, j, r0:r0 + CHUNK], start=c == 0, stop=False,
                                         skip_group_check=True)
                    last = nc.tensor.matmul(b4(d)[:, j, :], Vn[:, d, j, :], QKT[:, d, j, :], start=False, stop=True,
                                            skip_group_check=True)
                last.then_inc(S("o_ready"), 1)
        pe.wait_ge(S("o_sq"), n1(1, 1))
        for b in range(2):
            last = nc.tensor.matmul(banks[b][:, :], C("ones"), sq[:, 2 * b:2 * b + 2, :], start=True, stop=True)
        last.then_inc(S("o_ss"), 1)

    def state(tau, c):
        return Sv[:, (0, 1, 2, 0)[2 * tau + c]]

    def delta_act(act, it):
        for k in range(16):
            p = (first["delta"] + k, it, 16)
            act.wait_ge(S("panel_used"), at(p, 3))
            if k < 12:
                act.wait_ge(S("delta_done"), 1 + at((0, it, 1)))
                nc.scalar.copy(raw[:, k, 2:2 + T], pbank(p)).then_inc(S("proj_read"), 1)
            else:
                act.wait_ge(S("delta_done"), 1 + at((0, it, 1)))
                nc.scalar.activation(zg[:, k - 12, :], pbank(p), ACT.Silu).then_inc(S("proj_read"), 1)
            tick(act, act_split, p)
            if k < 12:
                act.wait_ge(S("convolved"), at((k + 1, it, 12)))
                nc.scalar.activation(qkv[:, k, :], qkv[:, k, :], ACT.Silu).then_inc(S("silued"), 1)
        n1 = lambda k, per: at((k, it, per))
        act.wait_ge(S("silued"), n1(12, 12))
        nc.scalar.activation(sq[:, 0:8, :], qkv[:, 0:8, :], ACT.Square).then_inc(S("qk_sq"), 1)
        act.wait_ge(S("qk_var"), n1(1, 1))
        nc.scalar.activation(sq[:, 8:16, :], sq[:, 8:16, :], ACT.Sqrt).then_inc(S("qk_std"), 1)
        act.wait_ge(S("kv_turned"), n1(1, 1))
        for t in range(TT):
            nc.scalar.copy(vtok[:, t], b4(t))
            last = nc.scalar.copy(ktok[:, t], b4(2 + t))
        last.then_inc(S("delta_ready"), 1)
        act.wait_ge(S("sums_ready"), n1(1, 1))
        nc.scalar.activation(esum, banks[4][:, 0:64].rearrange("p (k t d j) -> p k t d j", k=4, t=TT, d=2),
                             ACT.Exp).then_inc(S("esum_ready"), 1)
        act.wait_ge(S("esum_ready"), n1(1, 1))
        for tau in range(2):
            for d in range(2):
                act.wait_ge(S("pairs_ready"), at((tau * 2 + d + 1, it, 4)))
                nc.scalar.activation(qdec[:, d], b4(d), ACT.Exp).then_inc(S("edec_ready"), 1)
                act.wait_ge(S("diff_ready"), at((tau * 2 + d + 1, it, 4)))
                nc.scalar.activation(gam[:, d], gam[:, d], ACT.Exp).then_inc(S("gamma_ready"), 1)
            inv_act(act, (tau, it, 2), dinv)
            for d in range(2):
                ti = delta_tile(d, tau)
                act.wait_ge(S("xt_ready"), at((tau * 2 + d + 1, it, 4)))
                for j in range(4):
                    last = nc.scalar.activation(Kt[:, d, j, :], ktok[:, ti, j, :], ACT.Copy,
                                                scale=esum[:, 1, ti, d, j:j + 1])
                last.then_inc(S("kt_ready"), 1)
            for c in range(2):
                for d in range(2):
                    ti = delta_tile(d, tau)
                    r0 = CHUNK * (c if d == 0 else 1 - c)
                    rows = slice(0, P) if c == 0 else slice(r0, r0 + CHUNK)
                    act.wait_ge(S("w_ready"), at(((tau * 2 + c) * 2 + d + 1, it, 8)))
                    if c == 0 and d == 0:
                        act.wait_ge(S("kt_ready"), at((tau * 2 + 2, it, 4)))
                    for j in range(4):
                        last = nc.scalar.activation(Vn[rows, d, j, :], b4(2 + d)[rows, j, :], ACT.Copy,
                                                    scale=bcur[rows, ti, d, j:j + 1])
                    last.then_inc(S("vnew_ready"), 1)
        act.wait_ge(S("o_whole"), n1(1, 1))
        nc.scalar.activation(sq[:, 0:4, :], Oacc[:, :, :], ACT.Square).then_inc(S("o_sq"), 1)
        act.wait_ge(S("o_var"), n1(1, 1))
        nc.scalar.activation(sq[:, 4:8, :], sq[:, 4:8, :], ACT.Sqrt).then_inc(S("o_std"), 1)

    def delta_dve(dve, ch, it):
        ch(nc.vector.memset(raw[:, :, 0:2], 0.0))
        ch(nc.vector.memset(raw[:, :, T + 2:T + 4], 0.0))
        for k in range(16):
            p = (first["delta"] + k, it, 16)
            if k < 12:
                dve.wait_ge(S("proj_read"), at(p, 3))
                w = lambda j: cw_qkv[:, bass.ds(it * 60 + (k * 5 + j), 1)]
                if k == 0:
                    dve.wait_ge(S("delta_done"), 1 + at((0, it, 1)))
                ch(nc.vector.tensor_scalar(qkv[:, k, :], raw[:, k, 0:T], w(0), None, ALU.mult))
                for j in range(1, 5):
                    last = nc.vector.scalar_tensor_tensor(qkv[:, k, :], raw[:, k, j:j + T], w(j), qkv[:, k, :],
                                                          ALU.mult, ALU.add)
                    if j < 4:
                        ch(last)
                last.then_inc(S("convolved"), 1)
            tick(dve, dve_split, p)
        n1 = lambda k, per: at((k, it, per))
        i4 = lambda d: bass.ds(it * 4 + d * 8, 4)
        for d in range(2):
            nc.vector.tensor_copy(gcur[:, :, d, :], gates_f[:, :, i4(d)])
            nc.vector.tensor_copy(bcur[:, :, d, :], beta[:, :, i4(d)])
            last = nc.vector.tensor_scalar(nbcur[:, :, d, :], beta[:, :, i4(d)], -1.0, None, ALU.mult)
        last.then_inc(S("gcur_ready"), 1)
        dve.wait_ge(S("qk_ss"), n1(1, 1))
        for b in range(4):
            last = nc.vector.tensor_scalar(sq[:, 8 + 2 * b:10 + 2 * b, :], banks[b][:, :].rearrange("p (a t) -> p a t", a=2),
                                           EPS, None, ALU.add)
        last.then_inc(S("qk_var"), 1)
        dve.wait_ge(S("qk_std"), n1(1, 1))
        ch(nc.vector.reciprocal(sq[:, 8:16, :], sq[:, 8:16, :]))
        nc.vector.scalar_tensor_tensor(qkv[:, 0:4, :], qkv[:, 0:4, :], QSCALE, sq[:, 8:12, :], ALU.mult, ALU.mult)
        nc.vector.tensor_tensor(qkv[:, 4:8, :], qkv[:, 4:8, :], sq[:, 12:16, :], ALU.mult).then_inc(S("qk_normed"), 1)
        dve.wait_ge(S("qk_normed"), n1(1, 1))
        dve.wait_ge(S("esum_ready"), n1(1, 1))
        nc.vector.tensor_copy(sums, banks[4][:, 0:64].rearrange("p (k t d j) -> p k t d j", k=4, t=TT, d=2))
        ch(nc.vector.tensor_scalar(necum, esum[:, 0], -1.0, None, ALU.mult))
        nc.vector.memset(Sv[:, 0], 0.0).then_inc(S("delta_ready"), 1)
        dve.wait_ge(S("delta_ready"), n1(2, 2))
        dve.sem_inc(S("state_ready"), 2)
        for tau in range(2):
            for d in range(2):
                ti = delta_tile(d, tau)
                dve.wait_ge(S("edec_ready"), at((tau * 2 + d + 1, it, 4)))
                for j in range(4):
                    last = nc.vector.tensor_scalar(gam[:, d, j, :], b4(d)[:, j, :], sums[:, 0, ti, d, j:j + 1], 0.0,
                                                   ALU.subtract, ALU.min)
                last.then_inc(S("diff_ready"), 1)
                dve.wait_ge(S("gamma_ready"), at((tau * 2 + d + 1, it, 4)))
                ch(nc.vector.tensor_tensor(QKT[:, d], b4(4 + d), gam[:, d], ALU.mult))
                for j in range(4):
                    last = nc.vector.scalar_tensor_tensor(NT[:, d, j, :], b4(2 + d)[:, j, :], nbcur[:, ti, d, j:j + 1],
                                                          gam[:, d, j, :], ALU.mult, ALU.mult)
                last.then_inc(S("nt_raw"), 1)
                nc.vector.tensor_tensor(qdec[:, d], qdec[:, d], qkv[:, 0:4, ti * P:(ti + 1) * P], ALU.mult).then_inc(S("qdec_ready"), 1)
            inv_dve(dve, ch, (tau, it, 2), dinv)
            for c in range(2):
                nxt = (1, 2, 0, 1)[2 * tau + c]
                for d in range(2):
                    ti = delta_tile(d, tau)
                    r0 = CHUNK * (c if d == 0 else 1 - c)
                    rows = slice(0, P) if c == 0 else slice(r0, r0 + CHUNK)
                    dve.wait_ge(S("ks_ready"), at(((tau * 2 + c) * 2 + d + 1, it, 8)))
                    for j in range(4):
                        last = nc.vector.scalar_tensor_tensor(Rr[rows, d, j, :], b4(d)[rows, j, :],
                                                              necum[rows, ti, d, j:j + 1], vtok[rows, ti, j, :],
                                                              ALU.mult, ALU.add)
                    last.then_inc(S("r_ready"), 1)
                for d in range(2):
                    ti = delta_tile(d, tau)
                    ck = c if d == 0 else 1 - c
                    dve.wait_ge(S("ds_ready"), at(((tau * 2 + c) * 2 + d + 1, it, 8)))
                    for j in range(4):
                        last = nc.vector.scalar_tensor_tensor(Sv[:, nxt, d, j, :], state(tau, c)[:, d, j, :],
                                                              esum[:, 2 + ck, ti, d, j:j + 1], b4(4 + d)[:, j, :],
                                                              ALU.mult, ALU.add)
                    if tau == 0 or c == 0:
                        last.then_inc(S("state_ready"), 1)
                    else:
                        ch(last)
            for d in range(2):
                ti = delta_tile(d, tau)
                dve.wait_ge(S("o_ready"), at((tau * 2 + d + 1, it, 4)))
                o = Oacc[:, :, ti * P:(ti + 1) * P]
                if tau == 0:
                    nc.vector.tensor_copy(o, b4(d)).then_inc(S("o_read"), 1)
                else:
                    nc.vector.tensor_tensor(o, b4(d), o, ALU.add).then_inc(S("o_read"), 1)
        dve.wait_ge(S("o_read"), n1(4, 4))
        dve.sem_inc(S("o_whole"), 1)
        dve.wait_ge(S("o_ss"), n1(1, 1))
        for b in range(2):
            last = nc.vector.tensor_scalar(sq[:, 4 + 2 * b:6 + 2 * b, :], banks[b][:, :].rearrange("p (a t) -> p a t", a=2),
                                           1.0 / P, EPS, ALU.mult, ALU.add)
        last.then_inc(S("o_var"), 1)
        dve.wait_ge(S("o_std"), n1(1, 1))
        ch(nc.vector.reciprocal(sq[:, 4:8, :], sq[:, 4:8, :]))
        ch(nc.vector.tensor_tensor(sq[:, 4:8, :], Oacc[:, :, :], sq[:, 4:8, :], ALU.mult))
        nc.vector.scalar_tensor_tensor(mixed[:, bass.ds(it * 4, 4), :], sq[:, 4:8, :], dnorm, zg[:, :, :],
                                       ALU.mult, ALU.mult).then_inc(S("delta_done"), 1)

    def delta_pool(pool, it):
        for tau in range(2):
            for d in range(2):
                pool.wait_ge(S("nt_raw"), at((tau * 2 + d + 1, it, 4)))
                nc.gpsimd.tensor_tensor(NT[:, d], NT[:, d], bc(C("before", d)), ALU.mult).then_inc(S("nt_ready"), 1)
                nc.gpsimd.tensor_tensor(QKT[:, d], QKT[:, d], bc(C("upto", d)), ALU.mult).then_inc(S("qkt_ready"), 1)
            inv_pool(pool, (tau, it, 2), dinv)

    mask3 = place("mask3", D0, [P, TT, NBR, T])
    QK = [place(f"QK{u}", D0 + 6 + 6 * u, [P, 2 * NBR, T]) for u in range(2)]
    VC = [place(f"VC{u}", D0 + 18 + 3 * u, [P, NBR, T]) for u in range(2)]
    VT = [place(f"VT{u}", D0 + 24 + 3 * u, [P, NBR, TT, P]) for u in range(2)]
    Sc = [place(f"Sc{u}", D0 + 30 + 6 * u, [P, TT, NBR * T]) for u in range(2)]
    PT = [place(f"PT{u}", D0 + 42 + 6 * u, [P, NBR * TT, T]) for u in range(2)]
    cosb = place("cosb", D0 + 54, [32, T])
    sinb = place("sinb", D0 + 55, [32, T])
    rot = place("rot", D0 + 56, [32, 2, T])
    pos_i = place("pos_i", D0 + 58, [32, T], I32)
    pos_n = place("pos_n", D0 + 59, [32, T], I32)
    ang = place("ang", D0 + 60, [32, T])
    nf = place("nf", D0 + 61, [32, T])
    amax, arec, asum = stat[:, 0:4], stat[:, 4:8], stat[:, 8:12]
    PI = 3.1415925

    def angles_dve(dve, ch):
        dve.wait_ge(S("dil_loaded"), 32)
        ch(nc.vector.tensor_copy(ang[:, :], pos_i[:, :]))
        ch(nc.vector.tensor_scalar(ang[:, :], ang[:, :], one("freq")[0:32, :], None, ALU.mult))
        ch(nc.vector.tensor_scalar(nf[:, :], ang[:, :], 0.15915494309189535, None, ALU.mult))
        ch(nc.vector.tensor_copy(pos_n[:, :], nf[:, :]))
        ch(nc.vector.tensor_copy(nf[:, :], pos_n[:, :]))
        ch(nc.vector.scalar_tensor_tensor(ang[:, :], nf[:, :], -6.28125, ang[:, :], ALU.mult, ALU.add))
        ch(nc.vector.scalar_tensor_tensor(ang[:, :], nf[:, :], -0.0019353071795864769, ang[:, :], ALU.mult, ALU.add))
        ch(nc.vector.tensor_scalar(cosb[:, :], ang[:, :], 1.5707963267948966, None, ALU.add))
        for _ in range(2):
            ch(nc.vector.tensor_scalar(nf[:, :], cosb[:, :], PI, -6.283185307179586, ALU.is_gt, ALU.mult))
            ch(nc.vector.tensor_tensor(cosb[:, :], cosb[:, :], nf[:, :], ALU.add))
        ch(nc.vector.tensor_scalar(nf[:, :], ang[:, :], PI, -6.283185307179586, ALU.is_gt, ALU.mult))
        ch(nc.vector.tensor_tensor(sinb[:, :], ang[:, :], nf[:, :], ALU.add))
        ch(nc.vector.tensor_scalar(cosb[:, :], cosb[:, :], -PI, PI, ALU.max, ALU.min))
        nc.vector.tensor_scalar(sinb[:, :], sinb[:, :], -PI, PI, ALU.max, ALU.min).then_inc(S("angles"), 1)

    def angles_act(act):
        act.wait_ge(S("angles"), 1)
        nc.scalar.activation(cosb[:, :], cosb[:, :], ACT.Sin).then_inc(S("angles"), 1)
        nc.scalar.activation(sinb[:, :], sinb[:, :], ACT.Sin).then_inc(S("angles"), 1)
        act.wait_ge(S("x_loaded"), 32)
        nc.scalar.activation(CC, CC, ACT.Silu).then_inc(S("angles"), 1)

    def hd(it, u, per, k):
        return at((u * per + k, it, 2 * per))

    mod_ring = place("mod_ring", D0 + 62, [P, 2, KT * P])
    cond_in = place("cond_in", 204.5, [P, 2 * KT])
    CC = cond_in[:, :].rearrange("p (k c) -> p k c", c=2)
    MOD = place("MOD", 206.5, [P, 3 * KT, 2])

    def mod_index(u, k):
        return u * 6 + k // 3 * 2 + k % 3

    def mod_pe(pe, it, u, k, p):
        m = mod_index(u, k)
        pe.wait_ge(S("proj_read"), at(p, 1))
        pe.wait_ge(S(f"mod_loaded{m % 2}"), at((m, it, 12), 1, 2, 16))
        for t in range(KT):
            last = nc.tensor.matmul(banks[6 + p[0] % 2][:, T:T + 2], mod_ring[:, m % 2, t * P:(t + 1) * P], CC[:, t, :],
                                    start=t == 0, stop=t == KT - 1)
        last.then_inc(S("mod_used"), 1)

    def mod_act(act, it, u, k, p):
        nc.scalar.copy(MOD[:, bass.ds(it * 12 + mod_index(u, k), 1), :],
                       banks[6 + p[0] % 2][:, T:T + 2].rearrange("p (a c) -> p a c", a=1))

    def mod_load(sp, it, u, k):
        m = mod_index(u, k)
        sp.wait_ge(S("mod_used"), at((m, it, 12), 1))
        sp.dma_start(mod_ring[:, m % 2, :], a["w_mod"][bass.ds(it * 12 + m, 1), :, :]
                     .rearrange("a p c -> (a p) c")).then_inc(S(f"mod_loaded{m % 2}"), 16)

    def dil_pe(pe, it):
        def turn(u, b):
            pe.wait_ge(S("proj_read"), at((first["dil"] + u * 9 + 3 * b + 1, it, 18), 3))
            pe.wait_ge(S("roped"), 1 + hd(it, u, 3, b))
            pe.wait_ge(S("vtok_ready"), 1 + hd(it, u, 1, 0))
            nc.tensor.matmul(banks[5][0:64, :], C("turn", 0, 64)[0:32, :], QK[u][0:32, 2 * b:2 * b + 2, :],
                             start=True, stop=True).then_inc(S("turned"), 1)

        def v_rows(u):
            pe.wait_ge(S("proj_read"), at((first["dil"] + u * 9 + 8, it, 18), 3))
            pe.wait_ge(S("roped"), 1 + hd(it, u, 3, 3))
            pe.wait_ge(S("dil_out"), 1 + hd(it, u, 1, 0))
            for b in range(NBR):
                for t in range(TT):
                    m = 2 * b + t
                    last = nc.tensor.transpose(b4(4 + m // 4)[:, m % 4, :], VC[u][:, b, t * P:(t + 1) * P], C("ident"))
            last.then_inc(S("v_turned"), 1)

        def scores(u):
            pe.wait_ge(S("roped"), 1 + hd(it, u, 3, 3))
            pe.wait_ge(S("pt_ready"), 1 + hd(it, u, 2, 0))
            for q in range(TT):
                for b in range(NBR):
                    last = nc.tensor.matmul(banks[2 * q + b // 2][:, (b % 2) * T:(b % 2 + 1) * T],
                                            QK[u][:, 2 * b, q * P:(q + 1) * P], QK[u][:, 2 * b + 1, :],
                                            start=True, stop=True)
                last.then_inc(S("scored"), 1)

        def turn_p(u):
            for q in range(TT):
                pe.wait_ge(S("p_ready"), hd(it, u, 2, q + 1))
                for m in range(2 * NBR):
                    last = nc.tensor.transpose(b4(2 * q + m // 4)[:, m % 4, :], Sc[u][:, q, m * P:(m + 1) * P], C("ident"))
                last.then_inc(S("p_turned"), 1)

        def mix(u):
            pe.wait_ge(S("pt_ready"), 1 + hd(it, u, 2, 2))
            pe.wait_ge(S("vtok_ready"), 1 + hd(it, u, 1, 1))
            for m in range(2 * NBR):
                last = nc.tensor.matmul(banks[4][:, 0:T], VT[u][:, m // 2, m % 2, :], PT[u][:, m, :],
                                        start=m == 0, stop=m == 2 * NBR - 1)
            last.then_inc(S("dil_mixed"), 1)

        for u in range(2):
            for k in range(9):
                p = (first["dil"] + u * 9 + k, it, 18)
                if k % 3 < 2:
                    mod_pe(pe, it, u, k, p)
                project(pe, p, rhs_x, pbank(p))
                if k % 3 == 2:
                    turn(u, k // 3)
                if u == 1:
                    if k == 0:
                        scores(0)
                    if k == 3:
                        turn_p(0)
                    if k == 5:
                        mix(0)
            v_rows(u)
        scores(1)
        turn_p(1)
        mix(1)

    def dil_act(act, it):
        def exps(u):
            for q in range(TT):
                act.wait_ge(S("max_ready"), hd(it, u, 2, q + 1))
                nc.scalar.activation(Sc[u][:, q, :], Sc[u][:, q, :], ACT.Exp, bias=amax[:, 2 * u + q:2 * u + q + 1],
                                     accum_out=asum[:, 2 * u + q:2 * u + q + 1]).then_inc(S("exp_ready"), 1)

        def copy_p(u):
            for q in range(TT):
                act.wait_ge(S("p_turned"), hd(it, u, 2, q + 1))
                nc.scalar.copy(PT[u][:, 0:4, q * P:(q + 1) * P], b4(2 * q))
                nc.scalar.copy(PT[u][:, 4:6, q * P:(q + 1) * P], b4(2 * q + 1)[:, 0:2, :]).then_inc(S("pt_ready"), 1)

        for u in range(2):
            for k in range(9):
                p = (first["dil"] + u * 9 + k, it, 18)
                act.wait_ge(S("panel_used"), at(p, 3))
                dst = VC[u][:, k // 3, :] if k % 3 == 2 else QK[u][:, 2 * (k // 3) + k % 3, :]
                if k % 3 < 2:
                    mod_act(act, it, u, k, p)
                nc.scalar.copy(dst, pbank(p)).then_inc(S("proj_read"), 1)
                tick(act, act_split, p)
                if u == 1 and k == 1:
                    exps(0)
                if u == 1 and k == 3:
                    copy_p(0)
            act.wait_ge(S("v_turned"), hd(it, u, 1, 1))
            nc.scalar.copy(VT[u][:, 0:2].rearrange("p b t c -> p (b t) c"), b4(4))
            nc.scalar.copy(VT[u][:, 2], b4(5)[:, 0:2, :]).then_inc(S("vtok_ready"), 1)
        exps(1)
        copy_p(1)

    def dil_dve(dve, ch, it):
        def rope(u, b):
            dve.wait_ge(S("turned"), hd(it, u, 3, b + 1))
            wide = lambda ap: ap.rearrange("p (a t) -> p a t", a=1).to_broadcast([32, 2, T])
            qk = QK[u][0:32, 2 * b:2 * b + 2, :]
            nc.vector.tensor_tensor(rot[:, :, :], banks[5][0:32, :].rearrange("p (a t) -> p a t", a=2),
                                    wide(sinb[:, :]), ALU.mult)
            ch(nc.vector.tensor_tensor(qk, qk, wide(cosb[:, :]), ALU.mult))
            nc.vector.tensor_tensor(qk, qk, rot[:, :, :], ALU.add).then_inc(S("roped"), 1)

        def masked(u):
            for q in range(TT):
                dve.wait_ge(S("scored"), hd(it, u, 2, q + 1))
                mk = mask3[:, q].rearrange("p b t -> p (b t)")
                nc.vector.scalar_tensor_tensor(Sc[u][:, q, 0:512], banks[2 * q][:, :], QSCALE, mk[:, 0:512],
                                               ALU.mult, ALU.add)
                ch(nc.vector.scalar_tensor_tensor(Sc[u][:, q, 512:768], banks[2 * q + 1][:, 0:T], QSCALE,
                                                  mk[:, 512:768], ALU.mult, ALU.add))
                m = amax[:, 2 * u + q:2 * u + q + 1]
                ch(nc.vector.reduce_max(m, Sc[u][:, q, :], AX.X))
                nc.vector.tensor_scalar(m, m, -1.0, None, ALU.mult).then_inc(S("max_ready"), 1)

        def scaled(u):
            for q in range(TT):
                dve.wait_ge(S("exp_ready"), hd(it, u, 2, q + 1))
                r = arec[:, 2 * u + q:2 * u + q + 1]
                ch(nc.vector.reciprocal(r, asum[:, 2 * u + q:2 * u + q + 1]))
                nc.vector.tensor_scalar(Sc[u][:, q, :], Sc[u][:, q, :], r, None, ALU.mult).then_inc(S("p_ready"), 1)

        def put(u):
            dve.wait_ge(S("dil_mixed"), hd(it, u, 1, 1))
            nc.vector.tensor_copy(mixed[:, bass.ds(it * 2 + (HEADS + u), 1), :],
                                  banks[4][:, 0:T].rearrange("p (a t) -> p a t", a=1)).then_inc(S("dil_out"), 1)

        for u in range(2):
            for k in range(9):
                p = (first["dil"] + u * 9 + k, it, 18)
                tick(dve, dve_split, p)
                if k % 3 == 2:
                    rope(u, k // 3)
                if u == 1:
                    if k == 0:
                        masked(0)
                    if k == 1:
                        scaled(0)
                    if k == 5:
                        put(0)
        masked(1)
        scaled(1)
        put(1)

    def whole_act(act, c, src, sem):
        act.wait_ge(S(sem), c)
        nc.scalar.copy(x_hi[:, :, :], src[:, :, :]).then_inc(S("whole_hi"), 1)

    def whole_dve(dve, n, src):
        dve.wait_ge(S("whole_hi"), n)
        nc.vector.tensor_tensor(x_lo[:, :, :], src[:, :, :], x_hi[:, :, :].bitcast(F32), ALU.subtract).then_inc(S("whole_ready"), 1)

    def add_pe(pe, name, it):
        for k in range(2):
            p = (first[name] + k, it, 2)
            project(pe, p, rhs_x, pbank(p))

    def add_act(act, name, it):
        for k in range(2):
            p = (first[name] + k, it, 2)
            act.wait_ge(S("proj_read"), at(p, 3))
            tick(act, act_split, p)

    def add_dve(dve, name, it):
        for k in range(2):
            p = (first[name] + k, it, 2)
            dve.wait_ge(S("panel_used"), at(p, 3))
            xc = x[:, bass.ds(it * 2 + k, 1), :]
            nc.vector.tensor_tensor(xc, pbank(p).rearrange("p (a t) -> p a t", a=1), xc, ALU.add).then_inc(S("proj_read"), 1)
            tick(dve, dve_split, p)

    h_hi = place("h_hi", W0 + 16, [P, FT, T], FR)
    h_lo = place("h_lo", W0 + 60, [P, FT, T], FR)
    fraw = place("fraw", W0 + 104, [P, 2, 2, T + 2])
    fcv = place("fcv", W0 + 108.25, [P, 2, 2, T])

    def up_pe(pe, it):
        for k in range(4):
            p = (first["up"] + k, it, 4)
            project(pe, p, rhs_x, pbank(p))

    def up_act(act, it):
        for j in range(2):
            for g in range(2):
                p = (first["up"] + 2 * j + g, it, 4)
                act.wait_ge(S("panel_used"), at(p, 3))
                act.wait_ge(S("h_ready"), 1 + at((j, it, 2)))
                nc.scalar.copy(fraw[:, j, g, 1:1 + T], pbank(p)).then_inc(S("proj_read"), 1)
                tick(act, act_split, p)
            act.wait_ge(S("up_conv"), at((2 * j + 1, it, 4)))
            nc.scalar.activation(fcv[:, j, 0, :], fcv[:, j, 0, :], ACT.Silu).then_inc(S("up_silu"), 1)
            act.wait_ge(S("up_prod"), at((j + 1, it, 2)))
            nc.scalar.copy(h_hi[:, bass.ds(it * 2 + j, 1), :], fcv[:, j, 0:1, :]).then_inc(S("up_hi"), 1)

    def up_dve(dve, ch, it):
        for j in range(2):
            for g in range(2):
                p = (first["up"] + 2 * j + g, it, 4)
                tick(dve, dve_split, p)
                dve.wait_ge(S("proj_read"), at(p, 3))
                w = lambda c: cw_ffn[:, bass.ds(it * 12 + (j * 6 + g * 3 + c), 1)]
                ch(nc.vector.tensor_scalar(fcv[:, j, g, :], fraw[:, j, g, 0:T], w(0), None, ALU.mult))
                ch(nc.vector.scalar_tensor_tensor(fcv[:, j, g, :], fraw[:, j, g, 1:1 + T], w(1), fcv[:, j, g, :],
                                                  ALU.mult, ALU.add))
                nc.vector.scalar_tensor_tensor(fcv[:, j, g, :], fraw[:, j, g, 2:2 + T], w(2), fcv[:, j, g, :],
                                               ALU.mult, ALU.add).then_inc(S("up_conv"), 1)
            dve.wait_ge(S("up_silu"), at((j + 1, it, 2)))
            dve.wait_ge(S("up_conv"), at((2 * j + 2, it, 4)))
            nc.vector.tensor_tensor(fcv[:, j, 0, :], fcv[:, j, 0, :], fcv[:, j, 1, :], ALU.mult).then_inc(S("up_prod"), 1)
            dve.wait_ge(S("up_hi"), at((j + 1, it, 2)))
            nc.vector.tensor_tensor(h_lo[:, bass.ds(it * 2 + j, 1), :], fcv[:, j, 0:1, :],
                                    h_hi[:, bass.ds(it * 2 + j, 1), :].bitcast(F32), ALU.subtract).then_inc(S("h_ready"), 1)

    NC8, NP22 = 8, 22

    def down_pe(pe, it):
        for g in range(NC8 * FT):
            c, kt, k = g // FT, g % FT, g // KT
            s = (first["down"] + k) % 2
            p = (first["down"] + k, it, NP22)
            if g % KT == 0:
                pe.wait_ge(S("panel_split"), at(p, 3))
            if kt == 0:
                pe.wait_ge(S("down_read"), at((c, it, NC8), 1))
            o = banks[6 + c % 2][:, 0:T]
            hi, lo = (w[:, s, (g % KT) * P:(g % KT + 1) * P] for w in (w_hi, w_lo))
            nc.tensor.matmul(o, hi, h_hi[:, kt, :], start=kt == 0, stop=False)
            nc.tensor.matmul(o, hi, h_lo[:, kt, :], start=False, stop=False)
            last = nc.tensor.matmul(o, lo, h_hi[:, kt, :], start=False, stop=kt == FT - 1)
            if g % KT == KT - 1:
                last.then_inc(S("panel_used"), 1)
            if kt == FT - 1:
                if g % KT == KT - 1:
                    pe.wait_ge(S("panel_used"), at(p, 3))
                    pe.sem_inc(S("down_ready"), 1)
                else:
                    last.then_inc(S("down_ready"), 1)

    def down_act(act, it):
        for k in range(NP22):
            tick(act, act_split, (first["down"] + k, it, NP22))

    def down_dve(dve, it):
        c = 0
        for k in range(NP22):
            tick(dve, dve_split, (first["down"] + k, it, NP22))
            while c < NC8 and (c + 1) * FT <= (k + 1) * KT:
                dve.wait_ge(S("down_ready"), at((c + 1, it, NC8)))
                xc = x[:, bass.ds(it * NC8 + c, 1), :]
                nc.vector.tensor_tensor(xc, banks[6 + c % 2][:, 0:T].rearrange("p (a t) -> p a t", a=1), xc,
                                        ALU.add).then_inc(S("down_read"), 1)
                c += 1

    small2 = place("small2", 87.3125, [P, 480])
    s2 = lambda at_, n: small2[:, at_:at_ + n]
    G2, BM, GF2, PSC = s2(0, 16), s2(16, 48), s2(64, 16), s2(80, 8)
    MU, W0P, A0P = s2(88, 24), s2(112, 16), s2(128, 16)
    KKP, KAP, RKP, LGP, LBP = (s2(144 + 8 * k, 8) for k in range(5))
    GSC = s2(312, 32).rearrange("p (c k) -> p c k", c=2)
    MUI, MUH = s2(344, 24), s2(368, 24)
    KAI = s2(392, 8)
    NST = s2(400, 24)
    ELc = s2(424, 8).rearrange("p (d j c) -> p d j c", d=2, j=2)
    PAR = s2(440, 32)
    k_hi = place("k_hi", 108, [P, KT, T], FR)
    k_lo = place("k_lo", 124, [P, KT, T], FR)
    m_hi = place("m_hi", 108, [P, KT, T], FR)
    m_lo = place("m_lo", 124, [P, KT, T], FR)
    xc = place("xc", 140, [P, KT, T])
    B24 = place("B24", 140, [P, 3 * WT, T])
    sq2 = place("sq2", 168, [P, KT, T])
    rstd2 = place("rstd2", 184, [P, T])

    def norm2_pe(pe, c, src_sem_count):
        pe.wait_ge(S("sq_ready"), src_sem_count)
        for k in range(KT):
            last = nc.tensor.matmul(banks[0][:, 0:T], C("ones"), sq2[:, k, :], start=k == 0, stop=k == KT - 1)
        last.then_inc(S("ss_ready"), 1)

    def norm2_act(act, n, src, c, hi):
        if c:
            act.wait_ge(S("mod_split"), 1)
        nc.scalar.activation(sq2[:, :, :], src, ACT.Square).then_inc(S("sq_ready"), 1)
        act.wait_ge(S("var_ready"), n)
        nc.scalar.activation(rstd2[:, :], rstd2[:, :], ACT.Sqrt).then_inc(S("std_ready"), 1)
        if hi is not None:
            act.wait_ge(S("modulated"), c + 1)
            nc.scalar.copy(hi[:, :, :], sq2[:, :, :]).then_inc(S("mod_hi"), 1)

    def norm2_dve(dve, ch, n, src, c, hi, lo):
        dve.wait_ge(S("ss_ready"), n)
        nc.vector.tensor_scalar(rstd2[:, :], banks[0][:, 0:T], 1.0 / D, EPS, ALU.mult, ALU.add).then_inc(S("var_ready"), 1)
        dve.wait_ge(S("std_ready"), n)
        ch(nc.vector.reciprocal(rstd2[:, :], rstd2[:, :]))
        ch(nc.vector.tensor_tensor(sq2[:, :, :], src, rstd2[:, :].rearrange("p (a t) -> p a t", a=1).to_broadcast([P, KT, T]),
                                   ALU.mult))
        if hi is None:
            return
        for k in range(KT):
            last = nc.vector.tensor_scalar(sq2[:, k, :], sq2[:, k, :], GSC[:, c, k:k + 1], MOD[:, k, c:c + 1],
                                           ALU.mult, ALU.add)
        last.then_inc(S("modulated"), 1)
        dve.wait_ge(S("mod_hi"), c + 1)
        nc.vector.tensor_tensor(lo[:, :, :], sq2[:, :, :], hi[:, :, :].bitcast(F32), ALU.subtract).then_inc(S("mod_split"), 1)

    rhs_lc = lambda g, k: (x_hi[:, k, :], x_lo[:, k, :]) if g == 0 else (k_hi[:, k, :], k_lo[:, k, :])

    NAQ = [place(f"NAQ{u}", 164 + 5 * u, [P, T]) for u in range(2)]
    NAK = [place(f"NAK{u}", 165 + 5 * u, [P, 2 * T]) for u in range(2)]
    NAV = [place(f"NAV{u}", 167 + 5 * u, [P, 2 * T]) for u in range(2)]
    NVT = [place(f"NVT{u}", 174 + 2 * u, [P, 4, P]) for u in range(2)]
    NAG = [place(f"NAG{u}", 178 + u, [P, T]) for u in range(2)]
    NSc = place("NSc", 180, [P, 2, TT, 2 * T])
    NPT = place("NPT", 188, [P, 2, 4, T])
    NBI = [place(f"NBI{u}", 196 + 3 * u, [P, 2, 6 * GRID]) for u in range(2)]
    NCM = place("NCM", 202, [P, GRID])
    NSCALE = 64.0 ** -0.5

    def na_pe(pe, it):
        def v_rows(u):
            pe.wait_ge(S("proj_read"), at((first["na"] + u * 4 + 2, it, 8), 3))
            pe.wait_ge(S("nvt_ready"), 1 + hd(it, u, 1, 0))
            for t in range(4):
                last = nc.tensor.transpose(b4(4)[:, t, :], NAV[u][:, t * P:(t + 1) * P], C("ident"))
            last.then_inc(S("nv_turned"), 1)

        def scores(u):
            pe.wait_ge(S("proj_read"), at((first["na"] + u * 4 + 2, it, 8), 3))
            pe.wait_ge(S("npt_ready"), 1 + hd(it, u, 4, 0))
            for h in range(2):
                for q in range(TT):
                    r = slice(64 * h, 64 * h + 64)
                    nc.tensor.matmul(banks[2 * h + q][:, :], NAQ[u][r, q * P:(q + 1) * P], NAK[u][r, :],
                                     start=True, stop=True).then_inc(S("n_scored"), 1)

        def turn_p(u):
            for h in range(2):
                for q in range(TT):
                    pe.wait_ge(S("np_ready"), hd(it, u, 4, 2 * h + q + 1))
                    for m in range(4):
                        last = nc.tensor.transpose(b4(2 * h + q)[:, m, :], NSc[:, h, q, m * P:(m + 1) * P], C("ident"))
                    last.then_inc(S("np_turned"), 1)

        def mix(u):
            pe.wait_ge(S("npt_ready"), 1 + hd(it, u, 4, 4))
            pe.wait_ge(S("nvt_ready"), 1 + hd(it, u, 1, 1))
            pe.wait_ge(S("na_out"), 1 + hd(it, u, 1, 0))
            for h in range(2):
                for m in range(4):
                    last = nc.tensor.matmul(banks[5][64 * h:64 * h + 64, 0:T], NVT[u][:, m, 64 * h:64 * h + 64],
                                            NPT[:, h, m, :], start=m == 0, stop=m == 3)
            last.then_inc(S("na_mixed"), 1)

        for u in range(2):
            for k in range(4):
                p = (first["na"] + u * 4 + k, it, 8)
                if k in (1, 2):
                    project2(pe, p, rhs_lc, banks[6 + p[0] % 2])
                else:
                    project(pe, p, rhs_x, pbank(p))
                if u == 1:
                    if k == 0:
                        scores(0)
                    if k == 1:
                        turn_p(0)
                    if k == 2:
                        mix(0)
            v_rows(u)
        scores(1)
        turn_p(1)
        mix(1)

    def na_act(act, it):
        def exps(u):
            for h in range(2):
                for q in range(TT):
                    act.wait_ge(S("nmax_ready"), hd(it, u, 4, 2 * h + q + 1))
                    c = 2 * h + q
                    nc.scalar.activation(NSc[:, h, q, :], NSc[:, h, q, :], ACT.Exp, bias=NST[:, c:c + 1],
                                         accum_out=NST[:, 4 + c:5 + c]).then_inc(S("nexp_ready"), 1)

        def copy_p(u):
            for h in range(2):
                for q in range(TT):
                    act.wait_ge(S("np_turned"), hd(it, u, 4, 2 * h + q + 1))
                    nc.scalar.copy(NPT[:, h, :, q * P:(q + 1) * P], b4(2 * h + q)).then_inc(S("npt_ready"), 1)

        for u in range(2):
            for k in range(4):
                p = (first["na"] + u * 4 + k, it, 8)
                act.wait_ge(S("panel_used"), at(p, 3))
                if k == 3:
                    act.wait_ge(S("na_out"), 1 + at((u, it, 2)))
                    nc.scalar.activation(NAG[u][:, :], pbank(p), ACT.Silu).then_inc(S("proj_read"), 1)
                else:
                    nc.scalar.copy((NAQ, NAK, NAV)[k][u][:, :], pbank(p, (T, 2 * T, 2 * T)[k])).then_inc(S("proj_read"), 1)
                tick(act, act_split, p)
                if u == 1 and k == 0:
                    exps(0)
                if u == 1 and k == 1:
                    copy_p(0)
            act.wait_ge(S("nv_turned"), hd(it, u, 1, 1))
            nc.scalar.copy(NVT[u][:, :, :], b4(4)).then_inc(S("nvt_ready"), 1)
        exps(1)
        copy_p(1)

    def na_dve(dve, ch, it):
        def masked(u):
            for h in range(2):
                for q in range(TT):
                    c = 2 * h + q
                    dve.wait_ge(S("n_scored"), hd(it, u, 4, c + 1))
                    if h == 0 and q == 0:
                        dve.wait_ge(S("bias_ready"), hd(it, u, 1, 1))
                    nc.vector.scalar_tensor_tensor(NSc[:, h, q, 0:T], banks[2 * h + q][:, 0:T], NSCALE,
                                                   NBI[u][:, h, (2 - 2 * q) * GRID:(6 - 2 * q) * GRID], ALU.mult, ALU.add)
                    ch(nc.vector.tensor_scalar(NSc[:, h, q, T:2 * T], banks[2 * h + q][:, T:2 * T], NSCALE, None, ALU.mult))
                    ch(nc.vector.reduce_max(NST[:, c:c + 1], NSc[:, h, q, :], AX.X))
                    nc.vector.tensor_scalar(NST[:, c:c + 1], NST[:, c:c + 1], -1.0, None, ALU.mult).then_inc(S("nmax_ready"), 1)

        def scaled(u):
            for h in range(2):
                for q in range(TT):
                    c = 2 * h + q
                    dve.wait_ge(S("nexp_ready"), hd(it, u, 4, c + 1))
                    ch(nc.vector.reciprocal(NST[:, 8 + c:9 + c], NST[:, 4 + c:5 + c]))
                    nc.vector.tensor_scalar(NSc[:, h, q, :], NSc[:, h, q, :], NST[:, 8 + c:9 + c], None,
                                            ALU.mult).then_inc(S("np_ready"), 1)

        def put(u):
            dve.wait_ge(S("na_mixed"), hd(it, u, 1, 1))
            dve.wait_ge(S("proj_read"), at((first["na"] + u * 4 + 3, it, 8), 3))
            nc.vector.tensor_tensor(B24[:, bass.ds(it * 2 + u, 1), :], banks[5][:, 0:T].rearrange("p (a t) -> p a t", a=1),
                                    NAG[u][:, :].rearrange("p (a t) -> p a t", a=1), ALU.mult).then_inc(S("na_out"), 1)

        for u in range(2):
            for k in range(4):
                p = (first["na"] + u * 4 + k, it, 8)
                tick(dve, dve_split, p)
                if u == 1:
                    if k == 0:
                        masked(0)
                        scaled(0)
                    if k == 2:
                        put(0)
        masked(1)
        scaled(1)
        put(1)

    def na_pool(pool, it):
        for u in range(2):
            pool.wait_ge(S("na_out"), 1 + at((0, it, 2)))
            pool.dma_start(NBI[u][:, :, :], a["rpb"][bass.ds(it * 2 + u, 1), :, :, :].rearrange("a p h c -> (a p) h c")).then_inc(S(f"bias_loaded{u}"), 16)
            pool.wait_ge(S(f"bias_loaded{u}"), at((1, it, 1), 0, 1, 16))
            for h in range(2):
                v = NBI[u][:, h, :].rearrange("p (d c) -> p d c", d=6)
                last = nc.gpsimd.tensor_tensor(v, v, NCM[:, :].rearrange("p (a c) -> p a c", a=1).to_broadcast([P, 6, GRID]),
                                               ALU.add)
            last.then_inc(S("bias_ready"), 1)

    PM = place("PM", 164, [P, 4, TT, T])
    PWA = place("PWA", 172, [P, 4, TT, T])
    PW = place("PW", 180, [P, TT, T])
    PU = place("PU", 182, [P, TT, T])
    PG = place("PG", 184, [P, TT, T])
    PUT = place("PUT", 186, [P, TT, T])
    PDF = place("PDF", 188, [P, TT, T])

    def pool_pe(pe, it):
        for k in range(4):
            p = (first["pool"] + k, it, 4)
            project(pe, p, rhs_x, pbank(p))
        n = at((1, it, 1))
        pe.wait_ge(S("proj_read"), at((first["pool"] + 1, it, 4), 3))
        pe.wait_ge(S("pool_out"), 1 + at((0, it, 1)))
        for c in range(2):
            for t in range(TT):
                last = nc.tensor.transpose(banks[0][:, t * T + c * P:t * T + (c + 1) * P], PU[:, c, t * P:(t + 1) * P], C("ident"))
        last.then_inc(S("u_turned"), 1)
        pe.wait_ge(S("utok_ready"), n)
        for c in range(2):
            for t in range(TT):
                last = nc.tensor.matmul(banks[1 + c][:, 0:T], PUT[:, t, c * P:(c + 1) * P],
                                        PM[:, bass.ds(it, 1), t, :], start=t == 0, stop=t == 1)
        last.then_inc(S("pooled"), 1)
        pe.wait_ge(S("diff_copied"), n)
        pe.wait_ge(S("pw_ready"), n)
        for c in range(2):
            for t in range(2):
                last = nc.tensor.matmul(banks[3 + c][:, 0:T], PW[:, t, c * P:(c + 1) * P], PDF[:, t, :], start=t == 0, stop=t == 1)
        last.then_inc(S("pool_y"), 1)

    def pool_act(act, it):
        n = at((1, it, 1))
        for k in range(4):
            p = (first["pool"] + k, it, 4)
            act.wait_ge(S("panel_used"), at(p, 3))
            act.wait_ge(S("pool_out"), 1 + at((0, it, 1)))
            if k < 2:
                nc.scalar.copy(PU[:, k, :], pbank(p)).then_inc(S("proj_read"), 1)
            else:
                nc.scalar.activation(PG[:, k - 2, :], pbank(p), ACT.Silu).then_inc(S("proj_read"), 1)
            tick(act, act_split, p)
        act.wait_ge(S("u_turned"), n)
        nc.scalar.copy(PUT[:, :, :], banks[0][:, :].rearrange("p (t c) -> p t c", t=TT)).then_inc(S("utok_ready"), 1)
        act.wait_ge(S("pooled"), n)
        nc.scalar.copy(PDF[:, 0, :], banks[1][:, 0:T])
        nc.scalar.copy(PDF[:, 1, :], banks[2][:, 0:T]).then_inc(S("diff_copied"), 1)

    def pool_dve(dve, it):
        for k in range(4):
            tick(dve, dve_split, (first["pool"] + k, it, 4))
        dve.wait_ge(S("pool_y"), at((1, it, 1)))
        dve.wait_ge(S("proj_read"), at((first["pool"] + 3, it, 4), 3))
        for c in range(2):
            last = nc.vector.scalar_tensor_tensor(B24[:, bass.ds(it * 2 + (WT + c), 1), :],
                                                  banks[3 + c][:, 0:T].rearrange("p (a t) -> p a t", a=1),
                                                  PSC[:, bass.ds(it * 2 + c, 1)], PG[:, c:c + 1, :], ALU.mult, ALU.mult)
        last.then_inc(S("pool_out"), 1)

    def pool_pool(pool, it):
        pool.wait_ge(S("pool_out"), 1 + at((0, it, 1)))
        nc.gpsimd.tensor_copy(PW[:, :, :].rearrange("p (a t) c -> p a t c", a=1), PWA[:, bass.ds(it, 1), :, :]).then_inc(S("pw_ready"), 1)

    KA = place("KA", 164, [P, WT, 2 * T])
    VA = place("VA", 180, [P, WT, 2 * T])
    RA = place("RA", 196, [P, WT, T])
    LW = place("LW", 204, [P, 2 * T])

    def lora_pe(pe):
        p = (first["lora"], None, 0)
        project2(pe, p, rhs_lc, banks[6 + p[0] % 2])

    def lora_act(act):
        p = (first["lora"], None, 0)
        act.wait_ge(S("panel_used"), at(p, 3))
        nc.scalar.activation(LW[0:64, :], banks[6 + p[0] % 2][0:64, :], ACT.Tanh)
        nc.scalar.copy(LW[64:128, :], banks[6 + p[0] % 2][64:128, :]).then_inc(S("proj_read"), 1)
        tick(act, act_split, p)

    def kv_pe(pe, it):
        for k in range(2):
            p = (first["kv"] + k, it, 2)
            project2(pe, p, rhs_lc, banks[6 + p[0] % 2])

    def kv_act(act, it):
        for k in range(2):
            p = (first["kv"] + k, it, 2)
            act.wait_ge(S("panel_used"), at(p, 3))
            nc.scalar.copy((KA, VA)[k][:, bass.ds(it, 1), :],
                           pbank(p, 2 * T).rearrange("p (a t) -> p a t", a=1)).then_inc(S("proj_read"), 1)
            tick(act, act_split, p)

    def rg_pe(pe, it):
        for k in range(2):
            p = (first["rg"] + k, it, 2)
            project(pe, p, rhs_x, pbank(p))

    def rg_act(act, it):
        for k in range(2):
            p = (first["rg"] + k, it, 2)
            act.wait_ge(S("panel_used"), at(p, 3))
            src_ = pbank(p).rearrange("p (a t) -> p a t", a=1)
            if k == 0:
                nc.scalar.copy(RA[:, bass.ds(it, 1), :], src_).then_inc(S("proj_read"), 1)
            else:
                nc.scalar.activation(B24[:, bass.ds(it + 2 * WT, 1), :], src_, ACT.Silu).then_inc(S("proj_read"), 1)
            tick(act, act_split, p)

    def only_split(dve, name, per, it):
        for k in range(per):
            tick(dve, dve_split, (first[name] + k, it, per))

    spill_x = nc.dram_tensor("spill_x", [P, KT, T], F32, kind="Internal").ap()
    spill_hi = nc.dram_tensor("spill_hi", [P, KT, T], FR, kind="Internal").ap()
    spill_lo = nc.dram_tensor("spill_lo", [P, KT, T], FR, kind="Internal").ap()
    q4 = lambda name, kb: place(name, kb, [P, 2, 2, P])
    iv = lambda name, kb: place("r" + name, kb, [P, 2, 4, P])
    rinv = [iv(n_, kb) for n_, kb in (("NT", 48), ("N_", 52), ("A_", 56), ("AT", 60), ("B2", 64), ("B2T", 68),
                                      ("A4", 72), ("XT", 76), ("M_", 92))]
    rNT, rN, rA, rAT, rB2, rB2T, rA4, rXT, rM = rinv
    E0, E1, E2, Aa, Ld, Lc = (q4(n_, kb) for n_, kb in (("E0", 52), ("E1", 54), ("E2", 56), ("Aa", 58), ("Ld", 60), ("Lc", 62)))
    Vc = q4("Vc", 52)
    Kd = q4("Kd", 72)
    Tm = q4("Tm", 74)
    AakT = iv("AakT", 64)
    ArkT = iv("ArkT", 68)
    ArbT = iv("ArbT", 96)
    AT_, BT_, KT_, RT_ = (q4(n_, 100 + 2 * k) for k, n_ in enumerate(("a_t", "b_t", "k_t", "r_t")))
    Btok, Ktok, Vtok = (q4(n_, 108 + 2 * k) for k, n_ in enumerate(("Btok", "Ktok", "Vtok")))
    AV, RH, U_, YV = (q4(n_, 114 + 2 * k) for k, n_ in enumerate(("AV", "RH", "U_", "YV")))
    RS_ = place("RS_", 122, [P, 3, 4, P])
    KDs = place("KDs", 128, [P, 2, T])
    Y_ = place("Y_", 130, [P, 2, T])
    WA = q4("WA", 132)
    KK = place("KK", 134, [P, 2, 2 * T])
    Tb = place("Tb", 68, [P, 2, 2 * T])
    RK = place("RK", 48, [P, 2, 2 * T])
    RW = 4
    halves = lambda t: t[:, :, :, :].rearrange("p d j c -> p (d j) c")

    def r_tok(d, tau):
        return (T if tau < 2 else 0) + P * ((tau % 2) ^ d)

    def rstate(tau, c):
        return RS_[:, (2 * tau + c) % 3]

    def rw_params_dve(dve, ch):
        nc.vector.tensor_scalar(MUI, MU, -1.0, 1.0, ALU.mult, ALU.add)
        nc.vector.tensor_scalar(MUH, MU, 0.5, None, ALU.mult)
        ch(nc.vector.tensor_scalar(KAI, KAP, -1.0, 1.0, ALU.mult, ALU.add))

    def par(j, k, n=1):
        return PAR[:, j * 16 + k:j * 16 + k + n]

    def wa_pe(pe, it, tau):
        for d in range(2):
            for j in range(2):
                tk = r_tok(d, tau)
                for r, b in ((slice(0, 64), 6), (slice(64, 128), 7)):
                    last = nc.tensor.matmul(b4(b)[:, 2 * d + j, :], WA[r, d, j, :], LW[r, tk:tk + P], start=True, stop=True)
        last.then_inc(S("wa_mm"), 1)

    def rwkv_pe(pe, it):
        n = lambda k, per: at((k, it, per))
        pe.wait_ge(S("kk_step"), n(1, 4))
        for j in range(2):
            last = nc.tensor.matmul(banks[j][:, :], C("pairs"), RK[:, j, :], start=True, stop=True)
        last.then_inc(S("kk_step"), 1)
        pe.wait_ge(S("wa_ready"), at((1, it, 1), mul=16))
        wa_pe(pe, it, 0)
        for tau in range(4):
            sg = (RW + tau, it, 4)
            n4 = lambda k, per: at((tau * per + k, it, 4 * per))
            pe.wait_ge(S("tilde_ready"), n4(1, 1))
            for h in range(2):
                r = slice(64 * h, 64 * h + 64)
                for d in range(2):
                    for j in range(2):
                        m = 2 * d + j
                        nc.tensor.matmul(b4(h)[:, m, :], BT_[r, d, j, :], AT_[r, d, j, :], start=True, stop=True)
                        last = nc.tensor.matmul(b4(4 + h)[:, m, :], KT_[r, d, j, :], AT_[r, d, j, :], start=True, stop=True)
                        if tau >= 2:
                            last = nc.tensor.matmul(b4(2 + h)[:, m, :], BT_[r, d, j, :], RT_[r, d, j, :], start=True, stop=True)
                last.then_inc(S("pair_mm"), 1)
            if tau >= 2:
                for h in range(2):
                    r = slice(64 * h, 64 * h + 64)
                    pe.wait_ge(S("arb_ready"), at(((tau - 2) * 2 + h + 1, it, 4)))
                    for d in range(2):
                        for j in range(2):
                            last = nc.tensor.matmul(b4(2 + h)[:, 2 * d + j, :], KT_[r, d, j, :], RT_[r, d, j, :],
                                                    start=True, stop=True)
                    last.then_inc(S("ark_mm"), 1)
            pe.wait_ge(S("aak_ready"), n4(2, 2))
            for d in range(2):
                for j in range(2):
                    m = 2 * d + j
                    nc.tensor.transpose(b4(0)[:, m, :], BT_[:, d, j, :], C("ident"))
                    nc.tensor.transpose(b4(1)[:, m, :], KT_[:, d, j, :], C("ident"))
                    last = nc.tensor.transpose(b4(4)[:, m, :], Vc[:, d, j, :], C("ident"))
            last.then_inc(S("tok_mm"), 1)
            pe.wait_ge(S("tok_ready"), n4(1, 1))
            for h in range(2):
                for m in range(4):
                    last = nc.tensor.matmul(b4(5)[:, m, 64 * h:64 * h + 64], AakT[:, h, m, :],
                                            halves(Vtok)[:, m, 64 * h:64 * h + 64], start=True, stop=True)
            last.then_inc(S("av_mm"), 1)
            if tau >= 2:
                pe.wait_ge(S("ark_ready"), at(((tau - 2) * 2 + 2, it, 4)))
                for h in range(2):
                    for m in range(4):
                        last = nc.tensor.matmul(b4(4)[64 * h:64 * h + 64, m, :], halves(Vtok)[:, m, 64 * h:64 * h + 64],
                                                ArkT[:, h, m, :], start=True, stop=True)
                last.then_inc(S("yv_mm"), 1)
            if tau < 3:
                wa_pe(pe, it, tau + 1)
            pe.wait_ge(S("av_ready"), n4(1, 1))
            if tau >= 2:
                pe.wait_ge(S("yv_ready"), at((tau - 2 + 1, it, 2)))
            inv_pe(pe, sg, rinv)
            for c in range(2):
                nc8 = at((tau * 2 + c + 1, it, 8))
                if c == 0:
                    pe.wait_ge(S("xt_ready"), at((sg[0] * 2, it, 8), 2))
                pe.wait_ge(S("rs_ready"), nc8)
                for m in range(4):
                    last = nc.tensor.matmul(b4(0)[:, m, :], halves(AT_)[:, m, :], rstate(tau, c)[:, m, :], start=True, stop=True)
                last.then_inc(S("ap_mm"), 1)
                pe.wait_ge(S("rh_ready"), nc8)
                for h in range(2):
                    for m in range(4):
                        last = nc.tensor.matmul(b4(1)[:, m, 64 * h:64 * h + 64], rXT[:, h, m, :],
                                                halves(RH)[:, m, 64 * h:64 * h + 64], start=True, stop=True)
                last.then_inc(S("u_mm"), 1)
                pe.wait_ge(S("u_ready"), nc8)
                for d in range(2):
                    r0 = CHUNK * (c ^ d)
                    for j in range(2):
                        o = banks[2 + d][:, j * P:(j + 1) * P]
                        nc.tensor.matmul(o, Btok[r0:r0 + CHUNK, d, j, :], U_[r0:r0 + CHUNK, d, j, :], start=True, stop=False)
                        last = nc.tensor.matmul(o, Ktok[r0:r0 + CHUNK, d, j, :], Vtok[r0:r0 + CHUNK, d, j, :],
                                                start=False, stop=True)
                last.then_inc(S("rds_mm"), 1)
            if tau >= 2:
                for d in range(2):
                    for j in range(2):
                        m = 2 * d + j
                        for c in range(2):
                            r0 = CHUNK * (c ^ d)
                            nc.tensor.matmul(b4(4)[:, m, r0:r0 + CHUNK], rstate(tau, c)[:, m, :], RT_[:, d, j, r0:r0 + CHUNK],
                                             start=c == 0, stop=False, skip_group_check=True)
                        for h in range(2):
                            last = nc.tensor.matmul(b4(4)[64 * h:64 * h + 64, m, :], U_[:, d, j, 64 * h:64 * h + 64],
                                                    ArbT[:, h, m, :], start=False, stop=True, skip_group_check=True)
                last.then_inc(S("y_mm"), 1)
        pe.wait_ge(S("y_done"), n(2, 2))
        for j in range(2):
            last = nc.tensor.matmul(banks[0][:, j * T:(j + 1) * T], C("pairs"), Y_[:, j, :], start=True, stop=True)
        last.then_inc(S("mean_mm"), 1)
        pe.wait_ge(S("bonus_in"), n(1, 1))
        for j in range(2):
            last = nc.tensor.matmul(banks[2][:, j * T:(j + 1) * T], C("pairs"), KDs[:, j, :], start=True, stop=True)
        last.then_inc(S("bonus_mm"), 1)
        pe.wait_ge(S("ysq_ready"), n(1, 1))
        for j in range(2):
            last = nc.tensor.matmul(banks[1][:, j * T:(j + 1) * T], C("pairs"), RK[:, j, 0:T], start=True, stop=True)
        last.then_inc(S("var_mm"), 1)

    def sig_act(act, it, tau):
        act.wait_ge(S("wa_mm"), at((tau + 1, it, 4)))
        for d in range(2):
            for j in range(2):
                nc.scalar.activation(Ld[:, d, j, :], b4(6)[:, 2 * d + j, :], ACT.Sigmoid, bias=par(j, 6 + d))
                last = nc.scalar.activation(Aa[:, d, j, :], b4(7)[:, 2 * d + j, :], ACT.Sigmoid, bias=par(j, 8 + d))
        last.then_inc(S("sig_ready"), 1)

    def exps_act(act, it, tau):
        act.wait_ge(S("cum_ready"), at((tau + 1, it, 4)))
        nc.scalar.activation(E1[:, :, :, :], Lc[:, :, :, :], ACT.Exp)
        nc.scalar.activation(E2[:, :, :, :], Lc[:, :, :, :], ACT.Exp, scale=-1.0)
        nc.scalar.activation(E0[:, :, :, :], Tm[:, :, :, :], ACT.Exp).then_inc(S("exps_ready"), 1)

    def rwkv_act(act, it):
        n = lambda k, per: at((k, it, per))
        act.wait_ge(S("kk_in"), n(1, 1))
        nc.scalar.activation(RK[:, :, :], KK[:, :, :], ACT.Square).then_inc(S("kk_step"), 1)
        act.wait_ge(S("kk_step"), n(3, 4))
        nc.scalar.activation(RK[:, :, :], RK[:, :, :], ACT.Sqrt).then_inc(S("kk_step"), 1)
        sig_act(act, it, 0)
        exps_act(act, it, 0)
        for tau in range(4):
            sg = (RW + tau, it, 4)
            n4 = lambda k, per: at((tau * per + k, it, 4 * per))
            act.wait_ge(S("tok_mm"), n4(1, 1))
            nc.scalar.copy(halves(Btok), b4(0))
            nc.scalar.copy(halves(Ktok), b4(1))
            nc.scalar.copy(halves(Vtok), b4(4)).then_inc(S("tok_ready"), 1)
            act.wait_ge(S("av_mm"), n4(1, 1))
            nc.scalar.copy(halves(AV), b4(5)).then_inc(S("av_ready"), 1)
            if tau >= 2:
                act.wait_ge(S("yv_mm"), at((tau - 2 + 1, it, 2)))
                nc.scalar.copy(halves(YV), b4(4)).then_inc(S("yv_ready"), 1)
            inv_act(act, sg, rinv)
            if tau < 3:
                act.wait_ge(S("xt_ready"), at((sg[0] * 2, it, 8), 2))
                sig_act(act, it, tau + 1)
            for c in range(2):
                act.wait_ge(S("u_mm"), at((tau * 2 + c + 1, it, 8)))
                if c == 0:
                    nc.scalar.copy(halves(U_), b4(1)).then_inc(S("u_ready"), 1)
                    if tau < 3:
                        exps_act(act, it, tau + 1)
                else:
                    nc.scalar.copy(U_[64:128, 0, :, :], b4(1)[64:128, 0:2, :])
                    nc.scalar.copy(U_[0:64, 1, :, :], b4(1)[0:64, 2:4, :]).then_inc(S("u_ready"), 1)
        act.wait_ge(S("centred"), n(1, 1))
        nc.scalar.activation(RK[:, :, 0:T], Y_[:, :, :], ACT.Square).then_inc(S("ysq_ready"), 1)
        act.wait_ge(S("yvar_ready"), n(1, 1))
        nc.scalar.activation(RK[:, :, T:2 * T], RK[:, :, T:2 * T], ACT.Sqrt).then_inc(S("ystd_ready"), 1)

    def cum_dve(dve, ch, it, tau):
        dve.wait_ge(S("sig_ready"), at((tau + 1, it, 4)))
        ch(nc.vector.tensor_scalar(Ld[:, :, :, :], Ld[:, :, :, :], DECAY, None, ALU.mult))
        for d in range(2):
            for j in range(2):
                last = nc.vector.tensor_tensor_scan(Lc[:, d, j, :], C("carry"), Ld[:, d, j, :], 0.0, ALU.mult, ALU.add)
        ch(last)
        back = Lc[:, 1].rearrange("p j (c t) -> p (j c) t", t=CHUNK)
        ldb = Ld[:, 1].rearrange("p j (c t) -> p (j c) t", t=CHUNK)
        tmb = Tm[:, 1].rearrange("p j (c t) -> p (j c) t", t=CHUNK)
        nc.vector.tensor_tensor(Tm[:, 0], Lc[:, 0], Ld[:, 0], ALU.subtract)
        ch(nc.vector.tensor_tensor(tmb, back[:, :, CHUNK - 1:CHUNK].to_broadcast([P, 4, CHUNK]), back, ALU.subtract))
        nc.vector.tensor_tensor(back, tmb, ldb, ALU.add).then_inc(S("cum_ready"), 1)

    def keys_dve(dve, ch, it, tau):
        kcur = lambda t_, d: t_[:, :, r_tok(d, tau):r_tok(d, tau) + P]
        cur = lambda t_, d: t_[:, bass.ds(it * 2, 2), r_tok(d, tau):r_tok(d, tau) + P]
        dve.wait_ge(S("exps_ready"), at((tau + 1, it, 4)))
        for d in range(2):
            nc.vector.scalar_tensor_tensor(AT_[:, d], kcur(KK, d), -1.0, E0[:, d], ALU.mult, ALU.mult)
            nc.vector.tensor_tensor(BT_[:, d], kcur(KK, d), Aa[:, d], ALU.mult)
            for j in range(2):
                last = nc.vector.tensor_scalar(Kd[:, d, j], Aa[:, d, j], par(j, 11), par(j, 15), ALU.mult, ALU.add)
        ch(last)
        for d in range(2):
            nc.vector.tensor_tensor(Kd[:, d], Kd[:, d], cur(KA, d), ALU.mult)
            nc.vector.tensor_copy(Vc[:, d], cur(VA, d))
        ch(nc.vector.tensor_tensor(BT_[:, :, :, :], BT_[:, :, :, :], E2[:, :, :, :], ALU.mult))
        if tau >= 2:
            for d in range(2):
                o = KDs[:, :, r_tok(d, tau):r_tok(d, tau) + P]
                if tau == 2:
                    last = nc.vector.tensor_copy(o, Kd[:, d])
                else:
                    last = nc.vector.tensor_tensor(o, o, Kd[:, d], ALU.add)
            ch(last)
        ch(nc.vector.tensor_tensor(KT_[:, :, :, :], Kd[:, :, :, :], E2[:, :, :, :], ALU.mult))

    def tilde_dve(dve, it, tau):
        for d in range(2):
            end = E1[:, d].rearrange("p j (c t) -> p j c t", t=CHUNK)
            e = CHUNK - 1 if d == 0 else 0
            last = nc.vector.tensor_copy(ELc[:, d], end[:, :, :, e])
        if tau >= 2:
            for d in range(2):
                rr = RA[:, bass.ds(it * 2, 2), r_tok(d, tau):r_tok(d, tau) + P]
                last = nc.vector.tensor_tensor(RT_[:, d], rr, E1[:, d], ALU.mult)
        last.then_inc(S("tilde_ready"), 1)

    def rwkv_dve(dve, ch, it):
        n = lambda k, per: at((k, it, per))
        for j in range(2):
            for k, (t_, w, dyn) in enumerate(((MUI, 3, 3), (MUH, 3, 3), (W0P, 2, 2), (A0P, 2, 2))):
                o = (0, 3, 6, 8)[k]
                nc.vector.tensor_copy(par(j, o, w), t_[:, bass.ds(it * (2 * dyn) + j * dyn, w)])
            for k, t_ in enumerate((KKP, KAP, RKP, LGP, LBP, KAI)):
                last = nc.vector.tensor_copy(par(j, 10 + k), t_[:, bass.ds(it * 2 + j, 1)])
        ch(last)
        def shift(dst, w, j, which):
            nseq = w // T
            zi = dst[:, bass.ds(it * 2 + j, 1), :]
            z = zi.rearrange("p a (s t) -> p (a s) t", s=nseq)
            m = Tb[:, 0, 0:w].rearrange("p (s t) -> p s t", s=nseq)
            nc.vector.tensor_tensor(m[:, :, 1:T - 1], z[:, :, 0:T - 2], z[:, :, 2:T], ALU.add)
            nc.vector.tensor_copy(m[:, :, 0:1], z[:, :, 1:2])
            ch(nc.vector.tensor_copy(m[:, :, T - 1:T], z[:, :, T - 2:T - 1]))
            ch(nc.vector.tensor_scalar(z, z, par(j, which), None, ALU.mult))
            return z, m
        for j in range(2):
            z, m = shift(RA, T, j, 0)
            ch(nc.vector.scalar_tensor_tensor(z, m, par(j, 3), z, ALU.mult, ALU.add))
            for which, dst in ((1, KA), (2, VA)):
                z, m = shift(dst, 2 * T, j, which)
                ch(nc.vector.scalar_tensor_tensor(z, m, par(j, 3 + which), z, ALU.mult, ALU.add))
        for j in range(2):
            last = nc.vector.tensor_scalar(KK[:, j:j + 1, :], KA[:, bass.ds(it * 2 + j, 1), :], par(j, 10), None, ALU.mult)
        last.then_inc(S("kk_in"), 1)
        dve.wait_ge(S("kk_step"), n(2, 4))
        for j in range(2):
            last = nc.vector.tensor_copy(RK[:, j, :], banks[j][:, :])
        last.then_inc(S("kk_step"), 1)
        dve.wait_ge(S("kk_step"), n(4, 4))
        ch(nc.vector.tensor_scalar(RK[:, :, :], RK[:, :, :], 1e-12, None, ALU.max))
        ch(nc.vector.reciprocal(RK[:, :, :], RK[:, :, :]))
        ch(nc.vector.tensor_tensor(KK[:, :, :], KK[:, :, :], RK[:, :, :], ALU.mult))
        nc.vector.memset(RS_[:, 0], 0.0).then_inc(S("r_features"), 1)
        dve.wait_ge(S("r_features"), n(1, 1))
        dve.sem_inc(S("rs_ready"), 1)
        cum_dve(dve, ch, it, 0)
        keys_dve(dve, ch, it, 0)
        tilde_dve(dve, it, 0)
        for tau in range(4):
            sg = (RW + tau, it, 4)
            n4 = lambda k, per: at((tau * per + k, it, 4 * per))
            mk = lambda name: consts[:, cc[name][0]:cc[name][0] + 2 * P].rearrange("p (d a c) -> p d a c", d=2, a=1).to_broadcast([P, 2, 2, P])
            hv = lambda t_, h: t_[:, h].rearrange("p (d j) c -> p d j c", d=2)
            bk = lambda b: banks[b][:, :].rearrange("p (d j c) -> p d j c", d=2, j=2)
            for h in range(2):
                dve.wait_ge(S("pair_mm"), n4(h + 1, 2))
                if tau >= 2:
                    nc.vector.tensor_tensor(hv(ArbT, h), bk(2 + h), mk("upto"), ALU.mult).then_inc(S("arb_ready"), 1)
                nc.vector.tensor_tensor(hv(rNT, h), bk(h), mk("before"), ALU.mult).then_inc(S("nt_ready"), 1)
                nc.vector.tensor_tensor(hv(AakT, h), bk(4 + h), mk("before"), ALU.mult).then_inc(S("aak_ready"), 1)
            if tau >= 2:
                for h in range(2):
                    dve.wait_ge(S("ark_mm"), at(((tau - 2) * 2 + h + 1, it, 4)))
                    nc.vector.tensor_tensor(hv(ArkT, h), bk(2 + h), mk("upto"), ALU.mult).then_inc(S("ark_ready"), 1)
            inv_dve(dve, ch, sg, rinv)
            for c in range(2):
                nc8 = at((tau * 2 + c + 1, it, 8))
                dve.wait_ge(S("ap_mm"), nc8)
                if c == 0:
                    nc.vector.tensor_tensor(halves(RH), b4(0), halves(AV), ALU.add).then_inc(S("rh_ready"), 1)
                else:
                    nc.vector.tensor_tensor(RH[64:128, 0], b4(0)[64:128, 0:2, :], AV[64:128, 0], ALU.add)
                    nc.vector.tensor_tensor(RH[0:64, 1], b4(0)[0:64, 2:4, :], AV[0:64, 1], ALU.add).then_inc(S("rh_ready"), 1)
                if tau < 3:
                    (cum_dve, keys_dve)[c](dve, ch, it, tau + 1)
                dve.wait_ge(S("rds_mm"), nc8)
                nxt = RS_[:, (2 * tau + c + 1) % 3]
                for d in range(2):
                    last = nc.vector.tensor_tensor(nxt[:, 2 * d:2 * d + 2, :], banks[2 + d][:, 0:2 * P].rearrange("p (j c) -> p j c", j=2),
                                                   rstate(tau, c)[:, 2 * d:2 * d + 2, :], ALU.add)
                ch(last)
                for d in range(2):
                    for j in range(2):
                        m = nxt[:, 2 * d + j, :]
                        last = nc.vector.scalar_tensor_tensor(m, m, ELc[:, d, j, c ^ d:(c ^ d) + 1], C("pairs"), ALU.mult, ALU.mult)
                if tau == 3 and c == 1:
                    ch(last)
                else:
                    last.then_inc(S("rs_ready"), 1)
            if tau >= 2:
                dve.wait_ge(S("y_mm"), at((tau - 2 + 1, it, 2)))
                ch(nc.vector.tensor_tensor(halves(YV), b4(4), halves(YV), ALU.add))
            if tau < 3:
                dve.wait_ge(S("rs_ready"), at((tau * 2 + 3, it, 8)))
                tilde_dve(dve, it, tau + 1)
            if tau >= 2:
                for d in range(2):
                    o = Y_[:, :, r_tok(d, tau):r_tok(d, tau) + P]
                    if tau == 2:
                        last = nc.vector.tensor_copy(o, YV[:, d])
                    else:
                        last = nc.vector.tensor_tensor(o, o, YV[:, d], ALU.add)
                last.then_inc(S("y_done"), 1)
                dve.wait_ge(S("y_done"), at((tau - 2 + 1, it, 2)))
        dve.wait_ge(S("mean_mm"), n(1, 1))
        wide = lambda b: banks[b][:, :].rearrange("p (j t) -> p j t", j=2)
        nc.vector.scalar_tensor_tensor(Y_[:, :, :], wide(0), -1.0 / 64, Y_[:, :, :], ALU.mult, ALU.add).then_inc(S("centred"), 1)
        for j in range(2):
            last = nc.vector.scalar_tensor_tensor(KDs[:, j:j + 1, :], KDs[:, j:j + 1, :], par(j, 12),
                                                  RA[:, bass.ds(it * 2 + j, 1), :], ALU.mult, ALU.mult)
        last.then_inc(S("bonus_in"), 1)
        dve.wait_ge(S("bonus_mm"), n(1, 1))
        ch(nc.vector.tensor_tensor(KDs[:, :, :], wide(2), VA[:, bass.ds(it * 2, 2), 0:T], ALU.mult))
        dve.wait_ge(S("var_mm"), n(1, 1))
        nc.vector.tensor_scalar(RK[:, :, T:2 * T], wide(1), 1.0 / 64, LNX_EPS, ALU.mult, ALU.add).then_inc(S("yvar_ready"), 1)
        dve.wait_ge(S("ystd_ready"), n(1, 1))
        ch(nc.vector.reciprocal(RK[:, :, T:2 * T], RK[:, :, T:2 * T]))
        ch(nc.vector.tensor_tensor(Y_[:, :, :], Y_[:, :, :], RK[:, :, T:2 * T], ALU.mult))
        for j in range(2):
            last = nc.vector.tensor_scalar(Y_[:, j, :], Y_[:, j, :], par(j, 13), par(j, 14), ALU.mult, ALU.add)
        ch(last)
        ch(nc.vector.tensor_tensor(Y_[:, :, :], Y_[:, :, :], KDs[:, :, :], ALU.add))
        g = B24[:, bass.ds(it * 2 + 2 * WT, 2), :]
        nc.vector.tensor_tensor(g, g, Y_[:, :, :], ALU.mult).then_inc(S("rwkv_done"), 1)

    def rwkv_pool(pool, it):
        pool.wait_ge(S("rwkv_done"), 1 + at((0, it, 1)))
        pool.dma_start(WA[:, :, :, :], a["w2a2"][bass.ds(it, 1), :, :].rearrange("a p (d j c) -> (a p) d j c", d=2, j=2)).then_inc(S("wa_ready"), 16)
        for tau in range(4):
            inv_pool(pool, (RW + tau, it, 4), rinv)

    b_hi = place("b_hi", 164, [P, 3 * WT, T], FR)
    b_lo = place("b_lo", 140, [P, 3 * WT, T], FR)
    GL = place("GL", 188, [P, 2, 2, T])
    MG = place("MG", 192, [P, 2, T])
    MT_ = place("MT_", 194, [P, 2, T])
    wbank = lambda p: banks[6 + p[0] % 2][:, :].rearrange("p (o t) -> p o t", o=2)

    def branch_pe(pe, p, b):
        s = p[0] % 2
        pe.wait_ge(S("panel_split"), at(p, 3))
        pe.wait_ge(S("proj_read"), at(p, 1))
        for o in range(2):
            for k in range(WT):
                c = (o * WT + k) * P
                hi, lo = w_hi[:, s, c:c + P], w_lo[:, s, c:c + P]
                xh, xl = b_hi[:, b * WT + k, :], b_lo[:, b * WT + k, :]
                nc.tensor.matmul(wbank(p)[:, o, :], hi, xh, start=k == 0, stop=False)
                nc.tensor.matmul(wbank(p)[:, o, :], hi, xl, start=False, stop=False)
                last = nc.tensor.matmul(wbank(p)[:, o, :], lo, xh, start=False, stop=k == WT - 1)
        last.then_inc(S("panel_used"), 1)

    def merge_pe(pe, it):
        for k in range(18):
            p = (first["merge"] + k, it, 18)
            if k % 3 < 2:
                project(pe, p, rhs_x, pbank(p))
            else:
                branch_pe(pe, p, k // 3 % NBR)

    def merge_act(act, it):
        for k in range(18):
            p = (first["merge"] + k, it, 18)
            step_ = k // 3
            if k % 3 < 2:
                act.wait_ge(S("panel_used"), at(p, 3))
                if k % 3 == 0:
                    act.wait_ge(S("merge_step"), 1 + at((step_, it, 6)))
                nc.scalar.activation(GL[:, step_ % 2, k % 3, :], pbank(p), ACT.Sigmoid).then_inc(S("proj_read"), 1)
                tick(act, act_split, p)
            else:
                tick(act, act_split, p)
                act.wait_ge(S("proj_read"), at(p, 3))
            if k % 9 == 8:
                act.wait_ge(S("merge_step"), 2 + at((step_ + 1, it, 6)))
                nc.scalar.copy(m_hi[:, bass.ds(it * 4 + k // 9 * 2, 2), :], MG[:, :, :]).then_inc(S("merge_hi"), 1)

    def merge_dve(dve, ch, it):
        for k in range(18):
            p = (first["merge"] + k, it, 18)
            if k % 3 == 2:
                dve.wait_ge(S("panel_used"), at(p, 3))
                dve.wait_ge(S("proj_read"), at(p, 2))
                g = GL[:, k // 3 % 2]
                o = MG if k % 9 == 2 else MT_
                nc.vector.tensor_tensor(o[:, :, :], wbank(p), g, ALU.mult).then_inc(S("proj_read"), 1)
                dve.wait_ge(S("proj_read"), at(p, 3))
                if k % 9 > 2:
                    ch(nc.vector.tensor_tensor(MG[:, :, :], MG[:, :, :], MT_[:, :, :], ALU.add))
                dve.sem_inc(S("merge_step"), 1)
            tick(dve, dve_split, p)
            if k % 9 == 8:
                n = at((k // 9 + 1, it, 2))
                ds = bass.ds(it * 4 + k // 9 * 2, 2)
                dve.wait_ge(S("merge_hi"), n)
                nc.vector.tensor_tensor(m_lo[:, ds, :], MG[:, :, :], m_hi[:, ds, :].bitcast(F32),
                                        ALU.subtract).then_inc(S("merge_lo"), 1)
                dve.wait_ge(S("merge_lo"), n)

    def last_pe(pe, it, k0=0):
        for k in range(2):
            p = (first["wout2"] + k0 + k, it, 2)
            project(pe, p, lambda t: (m_hi[:, t, :], m_lo[:, t, :]), pbank(p))

    def last_act(act, it):
        for k in range(2):
            p = (first["wout2"] + k, it, 2)
            act.wait_ge(S("proj_read"), at(p, 3))
            tick(act, act_split, p)

    def last_dve(dve, it, k0=0, more=True):
        for k in range(2):
            p = (first["wout2"] + k0 + k, it, 2)
            dve.wait_ge(S("panel_used"), at(p, 3))
            if it is None:
                xt, gate = x[:, k0 + k:k0 + k + 1, :], MOD[:, 2 * KT + k0 + k, 0:1]
            else:
                xt, gate = x[:, bass.ds(it * 2 + k, 1), :], MOD[:, bass.ds(it * 2 + (2 * KT + k), 1), 0:1].rearrange("p a c -> p (a c)")
            nc.vector.scalar_tensor_tensor(xt, pbank(p).rearrange("p (a t) -> p a t", a=1), gate, xt,
                                           ALU.mult, ALU.add).then_inc(S("proj_read"), 1)
            if more:
                tick(dve, dve_split, p)

    block_cm = nc.Block()
    block = block_cm.__enter__()
    src = {"gates": "w_gates", "delta": "w_delta", "dil": "w_dil", "wout": "w_out", "up": "w_up", "down": "w_down",
           "na": "w_na", "pool": "w_pool", "lora": "w_lora", "kv": "w_kv", "rg": "w_rg", "wout2": "w_out2"}

    @block.sync
    def _(sp):
        def load(p, panel, w=KT * P):
            s = p[0] % 2
            sp.wait_ge(S("panel_split"), at(p, 1))
            sp.dma_start(ring[:, s, 0:w], panel).then_inc(S(f"panel_loaded{s}"), 16)

        def one_of(w, i):
            return w[bass.ds(i, 1), :, :].rearrange("a p c -> (a p) c")

        for name, per, trips in plan:
            if name == "merge":
                with sp.Fori(0, trips) as it:
                    for k in range(per):
                        w, i = (a["w_logit"], it * 12 + k // 3 * 2 + k % 3) if k % 3 < 2 else (a["w_branch"], it * 6 + k // 3)
                        load((first[name] + k, it, per), one_of(w, i))
            elif trips == 1:
                for k in range(per):
                    load((first[name] + k, None, 0), a[src[name]][k, :, :])
            else:
                with sp.Fori(0, trips) as it:
                    for k in range(per):
                        load((first[name] + k, it, per), one_of(a[src[name]], it * per + k))
                        if name == "dil" and k % 3:
                            mod_load(sp, it, (k - 1) // 9, (k - 1) % 9)

    @block.tensor
    def _(pe):
        pe.sem_inc(S("panel_used"), 2)
        pe.wait_ge(S("loaded0"), 32)
        norm_pe(pe, 1)
        pe.wait_ge(S("xsplit"), 1)
        gates_pe(pe)
        barrier(pe)
        with pe.Fori(0, 2) as it:
            delta_pe(pe, it)
        barrier(pe)
        pe.wait_ge(S("angles"), 4)
        pe.sem_inc(S("mod_used"), 2)
        with pe.Fori(0, 4) as it:
            dil_pe(pe, it)
        pe.wait_ge(S("whole_ready"), 1)
        with pe.Fori(0, 8) as it:
            add_pe(pe, "wout", it)
        barrier(pe)
        norm_pe(pe, 2)
        pe.wait_ge(S("xsplit"), 2)
        barrier(pe)
        with pe.Fori(0, 22) as it:
            up_pe(pe, it)
        pe.wait_ge(S("h_ready"), 1 + FT)
        with pe.Fori(0, 2) as it:
            down_pe(pe, it)
        barrier(pe)
        norm_pe(pe, 3)
        barrier(pe)
        norm2_pe(pe, 0, 4)
        norm2_pe(pe, 1, 5)
        barrier(pe)
        with pe.Fori(0, 4) as it:
            na_pe(pe, it)
        barrier(pe)
        pe.wait_ge(S("tables_loaded"), 48)
        with pe.Fori(0, 4) as it:
            pool_pe(pe, it)
        barrier(pe)
        lora_pe(pe)
        with pe.Fori(0, 8) as it:
            kv_pe(pe, it)
        with pe.Fori(0, 8) as it:
            rg_pe(pe, it)
        barrier(pe)
        barrier(pe)
        with pe.Fori(0, 4) as it:
            rwkv_pe(pe, it)
        barrier(pe)
        pe.wait_ge(S("spilled"), 96)
        pe.wait_ge(S("whole_ready"), 2)
        with pe.Fori(0, 4) as it:
            merge_pe(pe, it)
        pe.wait_ge(S("merge_lo"), KT // 2)
        with pe.Fori(0, 7) as it:
            last_pe(pe, it)
        last_pe(pe, None, 14)
        barrier(pe)
        norm2_pe(pe, 0, 6)

    @block.scalar
    def _(act):
        act.sem_inc(S("proj_read"), 2)
        act_split(act, (0, None, 0))
        act_split(act, (1, None, 0))
        act.wait_ge(S("x_loaded"), 32)
        act.wait_ge(S("loaded0"), 32)
        norm_act(act, 1, x[:, :, :])
        gain_act(act, 1, sq, g_mix)
        gates_act(act)
        barrier(act)
        with act.Fori(0, 2) as it:
            delta_act(act, it)
        barrier(act)
        angles_act(act)
        with act.Fori(0, 4) as it:
            dil_act(act, it)
        whole_act(act, 1 + HEADS, mixed, "dil_out")
        with act.Fori(0, 8) as it:
            add_act(act, "wout", it)
        barrier(act)
        norm_act(act, 2, x[:, :, :])
        gain_act(act, 2, sq, g_ffn)
        barrier(act)
        with act.Fori(0, 22) as it:
            up_act(act, it)
        act.wait_ge(S("proj_read"), first["down"] + 2)
        act.sem_inc(S("down_read"), 2)
        act.sem_inc(S("proj_read"), 2 * NP22)
        with act.Fori(0, 2) as it:
            down_act(act, it)
        barrier(act)
        norm_act(act, 3, x[:, :, :])
        barrier(act)
        norm2_act(act, 4, x[:, :, :], 0, x_hi)
        norm2_act(act, 5, xc[:, :, :], 1, k_hi)
        barrier(act)
        with act.Fori(0, 4) as it:
            na_act(act, it)
        barrier(act)
        with act.Fori(0, 4) as it:
            pool_act(act, it)
        barrier(act)
        lora_act(act)
        with act.Fori(0, 8) as it:
            kv_act(act, it)
        with act.Fori(0, 8) as it:
            rg_act(act, it)
        barrier(act)
        barrier(act)
        with act.Fori(0, 4) as it:
            rwkv_act(act, it)
        barrier(act)
        nc.scalar.copy(b_hi[:, :, :], B24[:, :, :]).then_inc(S("whole_hi"), 1)
        with act.Fori(0, 4) as it:
            merge_act(act, it)
        with act.Fori(0, 7) as it:
            last_act(act, it)
        barrier(act)
        norm2_act(act, 6, x[:, :, :], 0, None)

    @block.vector
    def _(dve):
        ch = Chain(dve, S("dve_chain"))
        dve.sem_inc(S("panel_split"), 2)
        dve_split(dve, (0, None, 0))
        dve_split(dve, (1, None, 0))
        dve.wait_ge(S("x_loaded"), 32)
        dve.wait_ge(S("loaded0"), 32)
        norm_dve(dve, ch, 1, x[:, :, :], sq[:, :, :])
        gain_dve(dve, ch, 1, sq, g_mix)
        gates_dve(dve, ch)
        barrier(dve)
        with dve.Fori(0, 2) as it:
            ch.enter(it, CHAIN["delta"])
            delta_dve(dve, ch, it)
            ch.leave(2)
        barrier(dve)
        angles_dve(dve, ch)
        dve.wait_ge(S("angles"), 3)
        with dve.Fori(0, 4) as it:
            ch.enter(it, CHAIN["dil"])
            dil_dve(dve, ch, it)
            ch.leave(4)
        whole_dve(dve, 1, mixed)
        with dve.Fori(0, 8) as it:
            add_dve(dve, "wout", it)
        barrier(dve)
        norm_dve(dve, ch, 2, x[:, :, :], sq[:, :, :])
        gain_dve(dve, ch, 2, sq, g_ffn)
        barrier(dve)
        ch(nc.vector.memset(fraw[:, :, :, 0:1], 0.0))
        ch(nc.vector.memset(fraw[:, :, :, T + 1:T + 2], 0.0))
        with dve.Fori(0, 22) as it:
            ch.enter(it, CHAIN["up"])
            up_dve(dve, ch, it)
            ch.leave(22)
        with dve.Fori(0, 2) as it:
            down_dve(dve, it)
        barrier(dve)
        norm_dve(dve, ch, 3, x[:, :, :], x[:, :, :])
        dve.wait_ge(S("normed"), 3)
        wide = lambda g: g.rearrange("p (k a) -> p k a", a=1).to_broadcast([P, KT, T])
        ch(nc.vector.tensor_tensor(x[:, :, :], x[:, :, :], wide(g_fin), ALU.mult))
        barrier(dve)
        dve.wait_ge(S("block2_loaded"), 32)
        ch(nc.vector.tensor_tensor(MOD[:, :, :], MOD[:, :, :], BM.rearrange("p (k a) -> p k a", a=1).to_broadcast([P, 3 * KT, 2]), ALU.add))
        for c in range(2):
            ch(nc.vector.scalar_tensor_tensor(GSC[:, c], MOD[:, KT:2 * KT, c], 1.0, G2, ALU.add, ALU.mult))
        norm2_dve(dve, ch, 4, x[:, :, :], 0, x_hi, x_lo)
        dve.wait_ge(S("block2_loaded"), 32)
        norm2_dve(dve, ch, 5, xc[:, :, :], 1, k_hi, k_lo)
        barrier(dve)
        with dve.Fori(0, 4) as it:
            ch.enter(it, CHAIN["na"])
            na_dve(dve, ch, it)
            ch.leave(4)
        barrier(dve)
        with dve.Fori(0, 4) as it:
            pool_dve(dve, it)
        barrier(dve)
        only_split(dve, "lora", 1, None)
        with dve.Fori(0, 8) as it:
            only_split(dve, "kv", 2, it)
        with dve.Fori(0, 8) as it:
            only_split(dve, "rg", 2, it)
        rw_params_dve(dve, ch)
        barrier(dve)
        barrier(dve)
        with dve.Fori(0, 4) as it:
            ch.enter(it, CHAIN["rwkv"])
            rwkv_dve(dve, ch, it)
            ch.leave(4)
        barrier(dve)
        dve.wait_ge(S("whole_hi"), 2)
        nc.vector.tensor_tensor(b_lo[:, :, :], B24[:, :, :], b_hi[:, :, :].bitcast(F32), ALU.subtract).then_inc(S("whole_ready"), 1)
        dve.sem_inc(S("merge_step"), 2)
        with dve.Fori(0, 4) as it:
            ch.enter(it, CHAIN["merge"])
            merge_dve(dve, ch, it)
            ch.leave(4)
        with dve.Fori(0, 7) as it:
            last_dve(dve, it)
        last_dve(dve, None, 14, False)
        barrier(dve)
        norm2_dve(dve, ch, 6, x[:, :, :], 0, None, None)
        nc.vector.tensor_tensor(sq2[:, :, :], sq2[:, :, :], wide(GF2), ALU.mult).then_inc(S("result"), 1)

    @block.gpsimd
    def _(pool):
        load_first(pool)
        for name in ("delta_done", "h_ready", "na_out", "pool_out", "rwkv_done",
                     "dil_out", "vtok_ready", "pt_ready", "nvt_ready", "npt_ready", "roped"):
            pool.sem_inc(S(name), 1)
        pool.dma_start(x[:, :, :], a["x"]).then_inc(S("x_loaded"), 16)
        pool.dma_start(cond_in[:, :], a["cond"]).then_inc(S("x_loaded"), 16)
        barrier(pool)
        with pool.Fori(0, 2) as it:
            delta_pool(pool, it)
        barrier(pool)
        pool.dma_start(mask3[:, :, :, :], a["mask3"]).then_inc(S("dil_loaded"), 16)
        pool.dma_start(pos_i[:, :], a["pos"]).then_inc(S("dil_loaded"), 16)
        barrier(pool)
        barrier(pool)
        barrier(pool)
        barrier(pool)
        pool.dma_start(small2[:, 0:184], a["small2"]).then_inc(S("block2_loaded"), 16)
        pool.dma_start(xc[:, :, :], a["ctx"]).then_inc(S("block2_loaded"), 16)
        pool.wait_ge(S("block2_loaded"), 32)
        barrier(pool)
        pool.dma_start(NCM[:, :], a["near"]).then_inc(S("tables_loaded"), 16)
        pool.wait_ge(S("tables_loaded"), 16)
        with pool.Fori(0, 4) as it:
            na_pool(pool, it)
        barrier(pool)
        pool.dma_start(PM[:, :, :, :], a["pool_m"]).then_inc(S("tables_loaded"), 16)
        pool.dma_start(PWA[:, :, :, :], a["pool_w"]).then_inc(S("tables_loaded"), 16)
        pool.wait_ge(S("tables_loaded"), 48)
        with pool.Fori(0, 4) as it:
            pool_pool(pool, it)
        barrier(pool)
        barrier(pool)
        for t, d in ((x, spill_x), (x_hi, spill_hi), (x_lo, spill_lo)):
            pool.dma_start(d, t[:, :, :]).then_inc(S("spilled"), 16)
        pool.wait_ge(S("spilled"), 48)
        barrier(pool)
        with pool.Fori(0, 4) as it:
            rwkv_pool(pool, it)
        barrier(pool)
        for t, d in ((x, spill_x), (x_hi, spill_hi), (x_lo, spill_lo)):
            pool.dma_start(t[:, :, :], d).then_inc(S("spilled"), 16)
        pool.wait_ge(S("spilled"), 96)
        barrier(pool)
        pool.wait_ge(S("result"), 1)
        pool.dma_start(out, sq2[:, :, :]).then_inc(S("stored"), 16)
        pool.wait_ge(S("stored"), 16)

    block_cm.__exit__(None, None, None)


CHAIN = {"delta": 64, "dil": 18, "up": 8, "na": 24, "rwkv": 72, "merge": 4}


def panels(w):
    k, c = w.shape
    return np.ascontiguousarray(w.reshape(k // P, P, c // P, P).transpose(2, 1, 0, 3)).reshape(c // P, P, k)


def per_channel(v):
    return np.ascontiguousarray(v.reshape(-1, P).T)


def host_arrays(i):
    o = {}
    o["consts"] = np.concatenate([np.asarray(c, np.float32) for c in constants().values()], 1)
    o["x"] = np.ascontiguousarray(i["x"][0].T.reshape(KT, P, T).transpose(1, 0, 2))
    w = i["w_in"][0]
    W = 1024
    gates = np.zeros((D, P), np.float32)
    gates[:, :32] = w[:, 4 * W:4 * W + 32]
    o["w_gates"] = panels(gates)
    q = panels(w[:, :4 * W])
    o["w_delta"] = np.concatenate([q[k * 8 + h * 4:k * 8 + h * 4 + 4] for h in range(2) for k in range(4)])
    q = panels(w[:, 4 * W + 32:]).reshape(3, NBR, HEADS, P, D)
    o["w_dil"] = q.transpose(2, 1, 0, 3, 4).reshape(HEADS * 9, P, D)
    o["w_out"] = panels(i["w_out"][0])
    q = panels(i["w_ffn_in"][0]).reshape(2, FT, P, D)
    o["w_up"] = q.transpose(1, 0, 2, 3).reshape(2 * FT, P, D)
    q = i["w_ffn_out"][0].reshape(FT, P, KT, P).transpose(2, 0, 1, 3).reshape(KT * FT // KT, KT, P, P)
    o["w_down"] = q.transpose(0, 2, 1, 3).reshape(FT, P, D)
    o["mask3"] = dilated_masks()
    o["pos"] = np.broadcast_to(i["positions"].reshape(1, T).astype(np.int32), (32, T))
    cw = i["conv_qkv_w"][0].T.reshape(3, 2, 4, P, 5).transpose(3, 1, 0, 2, 4).reshape(P, 120)
    cf = i["conv_ffn_w"][0].T.reshape(2, FT, P, 3).transpose(2, 1, 0, 3).reshape(P, FT * 6)
    rows = lambda v: np.broadcast_to(v.reshape(1, -1), (P, v.size))
    small = [per_channel(i["norm_mix_w"][0]), per_channel(i["norm_ffn_w"][0]), per_channel(i["norm_final_w"]), cw,
             rows(np.concatenate([i["a_log_fwd"][0], i["a_log_bwd"][0]])),
             rows(np.concatenate([i["dt_bias_fwd"][0], i["dt_bias_bwd"][0]])),
             i["delta_norm_w"][0].reshape(P, 1), cf]
    s = np.zeros((P, 470), np.float32)
    c = np.concatenate(small, 1)
    s[:, :c.shape[1]] = c
    o["small"] = s
    o["ctx"] = np.ascontiguousarray(i["ctx_2"][0].T.reshape(KT, P, T).transpose(1, 0, 2))
    o["w_mod"] = panels(i["w_mod_2"][0])
    w = panels(i["w_in_2"][0])
    part = lambda k: w[k * WT:(k + 1) * WT]
    zip4 = lambda *ps: np.stack(ps, 1).reshape(-1, P, D)
    o["w_na"] = zip4(part(0), part(1), part(2), part(3))
    u, g = part(4).reshape(4, 2, P, D), part(5).reshape(4, 2, P, D)
    o["w_pool"] = np.concatenate([u, g], 1).reshape(16, P, D)
    o["w_rg"] = zip4(part(6), part(9))
    o["w_kv"] = zip4(part(7), part(8))
    o["w_lora"] = w[10 * WT:10 * WT + 1]
    o["w_logit"] = w[10 * WT + 1:].reshape(NBR, KT // 2, 2, P, D).transpose(1, 0, 2, 3, 4).reshape(-1, P, D)
    q = np.stack([panels(i["w_branch_2"][0, b]) for b in range(NBR)], 0).reshape(NBR, KT // 2, 2, P, WT * P)
    o["w_branch"] = q.transpose(1, 0, 3, 2, 4).reshape(-1, P, D)
    o["w_out2"] = panels(i["w_out_2"][0])
    rpb = np.pad(i["na_rpb_2"][0], ((0, 0), (0, 0), (GRID - WIN, GRID - WIN)))
    o["rpb"] = np.stack([np.stack([rpb[:, 5 - r:11 - r, GRID - 1 - c:2 * GRID - 1 - c] for c in range(GRID)], 0)
                         for r in range(2)], 0).reshape(P, 8, 2, 6 * GRID).transpose(1, 0, 2, 3)
    o["near"] = near_columns()
    o["pool_m"] = pool_matrices()
    o["pool_w"] = i["pool_w_2"][0].reshape(4, TT, P, T).transpose(2, 0, 1, 3)
    w2 = np.concatenate([i["rw_w2_2"][0], i["rw_a2_2"][0]], 1)
    o["w2a2"] = w2.reshape(2, P, 4, 2, P).transpose(2, 1, 0, 3, 4).reshape(4, P, 4 * P)
    tiled = lambda v: v.reshape(v.shape[0], -1, P).transpose(2, 1, 0).reshape(P, -1)
    o["small2"] = np.concatenate([
        per_channel(i["norm_g_2"][0]), per_channel(i["b_mod_2"][0]), per_channel(i["final_g_2"]),
        per_channel(i["pool_scale_2"][0]), tiled(i["rw_mu_2"][0]), tiled(i["rw_w0_2"][0]), tiled(i["rw_a0_2"][0]),
        per_channel(i["rw_k_k_2"][0]), per_channel(i["rw_k_a_2"][0]), per_channel(i["rw_r_k_2"][0].reshape(-1)),
        per_channel(i["rw_lnx_g_2"][0]), per_channel(i["rw_lnx_b_2"][0])], 1)
    o["cond"] = tiled(np.stack([i["c_2"][0], i["c_ctx_2"]]))
    return {k: np.ascontiguousarray(v) for k, v in o.items()}


def kernel(**inputs):
    import concourse.bacc as bacc
    from concourse.bass_utils import run_bass_kernel_spmd

    arrays = host_arrays({k: np.asarray(v) for k, v in inputs.items()})
    nc = bacc.Bacc("TRN2", target_bir_lowering=False, num_devices=1)
    a = {k: nc.dram_tensor("in_" + k, v.shape, mybir.dt.from_np(v.dtype), kind="ExternalInput").ap()
         for k, v in arrays.items()}
    out = nc.dram_tensor("out", (P, KT, T), F32, kind="ExternalOutput").ap()
    program(nc, a, out)
    r = run_bass_kernel_spmd(nc, [{"in_" + k: v for k, v in arrays.items()}], core_ids=[0])
    y = r.results[0]["out"]
    return np.ascontiguousarray(y.transpose(2, 1, 0).reshape(1, T, D))
```
